# Optimizing a Trainium2 kernel written in Bass

```python
import jax, jax.numpy as jnp
from jax import lax
import numpy as np

D_MODEL = 1024
BATCH = 1
SEQ = 1024
DEPTH = 1

CHUNK = 64
N_MEM = 256
EPS = 1e-6
GDN_HEADS = 4
GDN_DK = 128
GDN_DV = 128
CONV_K = 4
DSA_HEADS = 8
DSA_HD = 64
IDX_HEADS = 16
IDX_HD = 64
TOPK_MAX = 256
XA_HEADS = 4
XA_HD = 128
D_FF = ((8 * D_MODEL + 3 * 256 - 1) // (3 * 256)) * 256

GDN_KEY_DIM = GDN_HEADS * GDN_DK
GDN_VAL_DIM = GDN_HEADS * GDN_DV
GDN_CONV_CH = 2 * GDN_KEY_DIM + GDN_VAL_DIM
DSA_DIM = DSA_HEADS * DSA_HD
IDX_Q_DIM = IDX_HEADS * IDX_HD
IN_SPLITS = (GDN_CONV_CH, GDN_VAL_DIM, GDN_HEADS, GDN_HEADS,
             DSA_DIM, DSA_DIM, DSA_DIM, IDX_Q_DIM, IDX_HD, IDX_HEADS)
D_IN = GDN_CONV_CH + GDN_VAL_DIM + 2 * GDN_HEADS + 3 * DSA_DIM + IDX_Q_DIM + IDX_HD + IDX_HEADS
D_MIX = GDN_VAL_DIM + DSA_DIM
XA_DIM = XA_HEADS * XA_HD

kernel_name = "hybrid_gdn_dsa_memxattn_block"

def rms_norm(x, g):
    xf = x.astype(jnp.float32)
    y = xf * lax.rsqrt(jnp.mean(xf * xf, axis=-1, keepdims=True) + EPS)
    return (y * g.astype(jnp.float32)).astype(x.dtype)

def l2norm(x):
    xf = x.astype(jnp.float32)
    return xf * lax.rsqrt(jnp.sum(xf * xf, axis=-1, keepdims=True) + EPS)

def split_cols(a, sizes):
    idx, s = [], 0
    for n in sizes[:-1]:
        s += n
        idx.append(s)
    return jnp.split(a, idx, axis=-1)

def alibi_slopes(n):
    return jnp.exp2(-8.0 * jnp.arange(1, n + 1, dtype=jnp.float32) / n)

def causal_conv(u, w):
    K, C = w.shape
    return lax.conv_general_dilated(u, w[:, None, :].astype(u.dtype), window_strides=(1,),
                                    padding=[(K - 1, 0)], dimension_numbers=('NWC', 'WIO', 'NWC'),
                                    feature_group_count=C)

def gated_delta_rule(q, k, v, g, beta):
    B, T, H, dk = q.shape
    dv = v.shape[-1]
    n = T // CHUNK

    def to_chunks(a):
        return jnp.moveaxis(a.reshape(B, n, CHUNK, *a.shape[2:]), 2, 3)

    qc, kc, vc = to_chunks(q), to_chunks(k), to_chunks(v)
    gc, bc = to_chunks(g), to_chunks(beta)
    decay = jnp.cumsum(gc, axis=-1)
    pos = jnp.arange(CHUNK)
    incl = pos[:, None] >= pos[None, :]
    strict = pos[:, None] > pos[None, :]
    diff = decay[..., :, None] - decay[..., None, :]
    gamma = jnp.exp(jnp.where(incl, diff, -jnp.inf))
    kb = kc * bc[..., None]
    vb = vc * bc[..., None]
    a_mat = jnp.where(strict, jnp.einsum('bnhid,bnhjd->bnhij', kb, kc) * gamma, 0.0)
    eye = jnp.eye(CHUNK, dtype=jnp.float32)
    t_mat = jax.lax.linalg.triangular_solve(eye + a_mat, jnp.broadcast_to(eye, a_mat.shape),
                                            left_side=True, lower=True)
    u = jnp.einsum('bnhij,bnhjd->bnhid', t_mat, vb)
    w = jnp.einsum('bnhij,bnhjd->bnhid', t_mat, kb * jnp.exp(decay)[..., None])
    qk = jnp.einsum('bnhid,bnhjd->bnhij', qc, kc) * gamma
    q_dec = qc * jnp.exp(decay)[..., None]
    k_dec = kc * jnp.exp(decay[..., -1:] - decay)[..., None]
    last = jnp.exp(decay[..., -1])

    def step(S, inp):
        qd, kd, u_, w_, qk_, l_ = inp
        v_new = u_ - jnp.einsum('bhcd,bhde->bhce', w_, S)
        o = jnp.einsum('bhcd,bhde->bhce', qd, S) + jnp.einsum('bhij,bhje->bhie', qk_, v_new)
        S = S * l_[..., None, None] + jnp.einsum('bhcd,bhce->bhde', kd, v_new)
        return S, o

    xs = tuple(jnp.moveaxis(a, 1, 0) for a in (q_dec, k_dec, u, w, qk, last))
    S0 = jnp.zeros((B, H, dk, dv), jnp.float32)
    _, o = lax.scan(step, S0, xs)
    o = jnp.moveaxis(jnp.moveaxis(o, 0, 1), 2, 3)
    return o.reshape(B, T, H, dv)

def gated_deltanet(qkv, z, b_logit, a_logit, conv_w, a_log, dt_bias, g_out):
    B, T, _ = qkv.shape
    qkv = jax.nn.silu(causal_conv(qkv, conv_w))
    q = l2norm(qkv[..., :GDN_KEY_DIM].reshape(B, T, GDN_HEADS, GDN_DK)) * (GDN_DK ** -0.5)
    k = l2norm(qkv[..., GDN_KEY_DIM:2 * GDN_KEY_DIM].reshape(B, T, GDN_HEADS, GDN_DK))
    v = qkv[..., 2 * GDN_KEY_DIM:].reshape(B, T, GDN_HEADS, GDN_DV).astype(jnp.float32)
    beta = jax.nn.sigmoid(b_logit.astype(jnp.float32))
    g = -jnp.exp(a_log.astype(jnp.float32)) * jax.nn.softplus(a_logit.astype(jnp.float32) + dt_bias.astype(jnp.float32))
    o = gated_delta_rule(q, k, v, g, beta)
    o = rms_norm(o, g_out) * jax.nn.silu(z.astype(jnp.float32).reshape(B, T, GDN_HEADS, GDN_DV))
    return o.reshape(B, T, GDN_VAL_DIM).astype(qkv.dtype)

def indexed_sparse_attention(q, k, v, q_idx, k_idx, w_idx, g_q, g_k):
    B, T, _ = q.shape
    topk = min(TOPK_MAX, T // 4)
    q = rms_norm(q.reshape(B, T, DSA_HEADS, DSA_HD), g_q)
    k = rms_norm(k.reshape(B, T, DSA_HEADS, DSA_HD), g_k).reshape(B, T, DSA_DIM)
    qi = q_idx.astype(jnp.float32).reshape(B, T, IDX_HEADS, IDX_HD)
    ki = k_idx.astype(jnp.float32)
    wi = w_idx.astype(jnp.float32) * (IDX_HEADS ** -0.5)
    slopes = alibi_slopes(DSA_HEADS)
    key_chunk = jnp.arange(T) // CHUNK

    def block(c):
        start = c * CHUNK
        qb = lax.dynamic_slice_in_dim(q, start, CHUNK, axis=1)
        qib = lax.dynamic_slice_in_dim(qi, start, CHUNK, axis=1)
        wib = lax.dynamic_slice_in_dim(wi, start, CHUNK, axis=1)
        dots = jnp.einsum('bqhd,bsd->bqhs', qib, ki) * (IDX_HD ** -0.5)
        score = jnp.einsum('bqh,bqhs->bqs', wib, jax.nn.relu(dots))
        admissible = key_chunk <= c
        score = jnp.where(admissible[None, None, :], score, -jnp.inf)
        _, sel = lax.top_k(score, topk)
        valid = admissible[sel]
        kg = jax.vmap(lambda kb, ib: kb[ib])(k, sel).reshape(B, CHUNK, topk, DSA_HEADS, DSA_HD)
        vg = jax.vmap(lambda vb, ib: vb[ib])(v, sel).reshape(B, CHUNK, topk, DSA_HEADS, DSA_HD)
        logits = jnp.einsum('bqhd,bqkhd->bhqk', qb, kg).astype(jnp.float32) * (DSA_HD ** -0.5)
        qpos = start + jnp.arange(CHUNK)
        dist = jnp.abs(qpos[None, :, None] - sel).astype(jnp.float32)
        logits = logits - slopes[None, :, None, None] * dist[:, None]
        logits = jnp.where(valid[:, None], logits, -jnp.inf)
        p = jax.nn.softmax(logits, axis=-1)
        out = jnp.einsum('bhqk,bqkhd->bqhd', p.astype(vg.dtype), vg)
        return out.reshape(B, CHUNK, DSA_DIM)

    outs = lax.map(block, jnp.arange(T // CHUNK))
    return jnp.moveaxis(outs, 0, 1).reshape(B, T, DSA_DIM)

def memory_cross_attention(h, m, w_q, w_kv, w_o, g_q, g_k):
    B, T, _ = h.shape
    M = m.shape[1]
    q = rms_norm((h @ w_q).reshape(B, T, XA_HEADS, XA_HD), g_q)
    k, v = jnp.split(m @ w_kv, 2, axis=-1)
    k = rms_norm(k.reshape(B, M, XA_HEADS, XA_HD), g_k)
    v = v.reshape(B, M, XA_HEADS, XA_HD)
    logits = jnp.einsum('bthd,bmhd->bhtm', q, k).astype(jnp.float32) * (XA_HD ** -0.5)
    p = jax.nn.softmax(logits, axis=-1)
    o = jnp.einsum('bhtm,bmhd->bthd', p.astype(v.dtype), v).reshape(B, T, XA_DIM)
    return o @ w_o

def setup_inputs(seed: int = 0) -> dict:
    key = jax.random.key(seed)
    ks = jax.random.split(key, 24)
    f32 = jnp.float32

    def dense(k, fan_in, fan_out):
        return jax.random.normal(k, (DEPTH, fan_in, fan_out), f32) * fan_in ** -0.5

    def gain(k, n):
        return 1.0 + 0.02 * jax.random.normal(k, (DEPTH, n), f32)

    x = jax.random.normal(ks[0], (BATCH, SEQ, D_MODEL), f32)
    mem = jax.random.normal(ks[1], (BATCH, N_MEM, D_MODEL), f32)
    dt = jnp.exp(jax.random.uniform(ks[6], (DEPTH, GDN_HEADS), f32, np.log(1e-3), np.log(1e-1)))
    return {
        "x": x,
        "mem": mem,
        "g_mix": gain(ks[2], D_MODEL),
        "w_in": dense(ks[3], D_MODEL, D_IN),
        "conv_w": jax.random.normal(ks[4], (DEPTH, CONV_K, GDN_CONV_CH), f32) * CONV_K ** -0.5,
        "a_log": jnp.log(jax.random.uniform(ks[5], (DEPTH, GDN_HEADS), f32, 1.0, 16.0)),
        "dt_bias": dt + jnp.log(-jnp.expm1(-dt)),
        "g_gdn_out": gain(ks[7], GDN_DV),
        "g_q_dsa": gain(ks[8], DSA_HD),
        "g_k_dsa": gain(ks[9], DSA_HD),
        "w_out": dense(ks[10], D_MIX, D_MODEL),
        "g_xattn": gain(ks[11], D_MODEL),
        "g_mem": gain(ks[12], D_MODEL),
        "w_xq": dense(ks[13], D_MODEL, XA_DIM),
        "w_xkv": dense(ks[14], D_MODEL, 2 * XA_DIM),
        "g_xq": gain(ks[15], XA_HD),
        "g_xk": gain(ks[16], XA_HD),
        "w_xo": dense(ks[17], XA_DIM, D_MODEL),
        "g_ffn": gain(ks[18], D_MODEL),
        "w_gu": dense(ks[19], D_MODEL, 2 * D_FF),
        "w_down": dense(ks[20], D_FF, D_MODEL),
    }

def reference(x, mem, g_mix, w_in, conv_w, a_log, dt_bias, g_gdn_out, g_q_dsa, g_k_dsa, w_out,
              g_xattn, g_mem, w_xq, w_xkv, g_xq, g_xk, w_xo, g_ffn, w_gu, w_down):
    for l in range(DEPTH):
        h = rms_norm(x, g_mix[l])
        proj = h @ w_in[l]
        (gdn_qkv, gdn_z, gdn_b, gdn_a, dsa_q, dsa_k, dsa_v,
         idx_q, idx_k, idx_w) = split_cols(proj, IN_SPLITS)
        y_a = gated_deltanet(gdn_qkv, gdn_z, gdn_b, gdn_a, conv_w[l], a_log[l], dt_bias[l], g_gdn_out[l])
        y_b = indexed_sparse_attention(dsa_q, dsa_k, dsa_v, idx_q, idx_k, idx_w, g_q_dsa[l], g_k_dsa[l])
        x = x + jnp.concatenate([y_a, y_b], axis=-1) @ w_out[l]
        h = rms_norm(x, g_xattn[l])
        m = rms_norm(mem, g_mem[l])
        x = x + memory_cross_attention(h, m, w_xq[l], w_xkv[l], w_xo[l], g_xq[l], g_xk[l])
        h = rms_norm(x, g_ffn[l])
        gate, up = jnp.split(h @ w_gu[l], 2, axis=-1)
        x = x + (jax.nn.silu(gate) * up) @ w_down[l]
    return x


_drawn_inputs = setup_inputs


def setup_inputs(seed=0):
    import zlib

    import numpy as np

    out = dict(_drawn_inputs(seed))
    spreads = {}
    factors = {'g_gdn_out': 6.555,
     'g_q_dsa': 8.0,
     'g_k_dsa': 8.0,
     'g_xattn': 8.0,
     'g_mem': 8.0,
     'g_xq': 8.0,
     'g_xk': 8.0,
     'g_ffn': 4.264}
    for name, (base, spread) in spreads.items():
        noise = np.random.default_rng([zlib.crc32(name.encode()), seed]).standard_normal(out[name].shape)
        drawn = base * np.exp(spread * noise) if base else spread * noise
        out[name] = __import__('jax').numpy.asarray(drawn.astype(out[name].dtype))
    for name, factor in factors.items():
        out[name] = (out[name] * factor).astype(out[name].dtype)
    return out
```

```python
from contextlib import ExitStack

import concourse.bass as bass
from concourse import mybir

F32 = mybir.dt.float32
F32R = mybir.dt.float32r
ALU = mybir.AluOpType
ACT = mybir.ActivationFunctionType
AX = mybir.AxisListType.X

P = 128
SEQ, D, N_MEM = 1024, 1024, 256
CHUNK = 64
KT = D // P
TT = SEQ // P
BANK = 512
HALVES = SEQ // BANK
EPS = 1e-6
GH, GD = 4, 128
SH, SD = 8, 64
IH = 16
TOPK = 256
XH = 4
D_FF = 2816
KB = 1024
BIG = 1e30
TAKEN = -3e38
N_SMALL = 88

C_QKV, C_Z, C_B, C_DQ, C_DK, C_DV, C_IQ, C_IK = 0, 1536, 2048, 2056, 2568, 3080, 3592, 4616

EOFF = [P * t * (t + 1) // 2 for t in range(TT + 1)]
PAIRS = [(7, 2), (6, 3), (5, 4)]
ROUNDS = TOPK // 8
FFG = D_FF // 256
RING = 3


class Steps:

    def __init__(self, sem, names):
        self.sem, self.names, self.n = sem, list(names), 0
        self.at = {x: i + 1 for i, x in enumerate(self.names)}

    def value(self, name, rnd=0):
        return rnd * len(self.names) + self.at[name]

    def mark(self, ins, name, rnd=0):
        self.n += 1
        assert self.n == self.value(name, rnd), (name, rnd, self.n)
        ins.then_inc(self.sem, 1)
        return ins

    def wait(self, eng, name, rnd=0):
        eng.wait_ge(self.sem, self.value(name, rnd))


def chunks(n):
    return [(c, min(BANK, n - c)) for c in range(0, n, BANK)]


def build_layer(nc, x, mem, g_mix, w_in, conv_w, a_log, dt_bias, g_gdn_out, g_q_dsa, g_k_dsa, w_out,
                g_xattn, g_mem, w_xq, w_xkv, g_xq, g_xk, w_xo, g_ffn, w_gu, w_down, out):
    ctx = ExitStack()
    with ctx:
        base = (nc.sbuf_base + 63) // 64 * 64

        def at(name, shape, kb, dt=F32):
            return nc.alloc_sbuf_tensor_at(name, shape, dt, offset=base + int(kb * KB))

        def sem(name):
            return ctx.enter_context(nc.semaphore(name))

        def steps(name, names):
            return Steps(sem(name), names)

        ps = ctx.enter_context(nc.psum_tensor("ps", [P, 8, BANK], F32))
        z_dram = nc.dram_tensor("z_spill", (GH, P, SEQ), F32, kind="Internal").ap()
        d_dram = nc.dram_tensor("dsa_spill", (12, P, SEQ), F32, kind="Internal").ap()

        cur = [0.0]

        def small(name, cols):
            t = at(name, [P, cols], cur[0])
            cur[0] += (cols * 4 + 31) // 32 * 32 / KB
            return t

        ident = small("ident", P)
        Ublk = small("Ublk", P)
        Mblk = small("Mblk", P)
        Us = small("Us", CHUNK)
        Ms = small("Ms", CHUNK)
        I64 = small("I64", CHUNK)
        Lev = small("Lev", 6 * CHUNK)
        negdist = small("negdist", SEQ)
        gB = small("gB", D)
        half_ones = small("half_ones", 2 * P)
        blk2 = small("blk2", 2)
        ones1 = small("ones1", 2)
        zero1 = small("zero1", 2)
        eps_t = small("eps_t", 2)
        wba = small("wba", TT * 24)
        top8 = small("top8", 16)
        ss = small("ss", 128)
        sd = small("sd", 128)
        rs = small("rs", 128)
        beta = small("beta", 32)
        gdec = small("gdec", 32)
        nbed = small("nbed", 32)
        erem = small("erem", 32)
        lastb = small("lastb", 64)
        gtmp = small("gtmp", 32 * 4)
        dtB = small("dtB", 4)
        alB = small("alB", 4)
        sm8 = small("sm8", 64)
        stage = small("stage", P)
        cols_t = small("cols_t", 56)
        assert cur[0] <= 20, cur[0]

        WR = at("WR", [P, RING, 1024], 20)
        WS = at("WS", [P, RING, 2, 1024], 32, F32R)
        HS = at("HS", [P, 2, KT, SEQ], 56, F32R)

        X = at("X", [P, TT, D], 120)
        xn = at("xn", [P, 2, D], 152)
        junk = at("junk", [P, 2, D], 160)
        score = at("score", [P, EOFF[TT]], 168)
        qI = at("qI", [P, 2, 2, SEQ], 124, F32R)
        kI = at("kI", [P, 2, SEQ], 186, F32R)
        relu = at("relu", [P, 3, BANK], 198)
        wT = at("wT", [24, SEQ], 120)
        QKV = at("QKV", [P, 12, SEQ], 120)
        raw = at("raw", [P, 2, SEQ + 4], 186)
        cacc = at("cacc", [P, 2, SEQ], 195)
        sqg = at("sqg", [P, 8, SEQ], 56)
        kdec = at("kdec", [P, 2, 8 * P], 56)
        vb = at("vb", [P, 2, 8 * P], 64)
        wTt = at("wTt", [P, 2, 8 * P], 72)
        qdec = at("qdec", [P, 2, 8 * P], 80)
        TTm = at("TTm", [P, 2, BANK], 88)
        QKm = at("QKm", [P, 2, BANK], 92)
        nkbd = at("nkbd", [P, 8 * P], 96)
        Tm = at("Tm", [P, BANK], 100)
        Xm = at("Xm", [P, BANK], 102)
        Ym = at("Ym", [P, BANK], 104)
        Am = at("Am", [P, BANK], 106)
        gam = at("gam", [P, 2, BANK], 108)
        gMU = at("gMU", [P, 2, BANK], 112)
        S = at("S", [P, 2, BANK], 116)
        yA = at("yA", [P, 4, SEQ], 186)
        Sl = at("Sl", [P, BANK], 202)
        vn = at("vn", [P, BANK], 204)
        zS = at("zS", [P, 4, SEQ], 152)
        qD = at("qD", [P, 4, SEQ], 100)
        qO = at("qO", [P, 4, SEQ], 116)
        kD = at("kD", [P, 4, SEQ], 136)
        sqh = at("sqh", [P, 2, BANK], 96)
        vraw = at("vraw", [P, 4, SEQ], 186)
        yB = at("yB", [P, 4, SEQ], 152)
        vtok = at("vtok", [P, TT, BANK], 56)
        L = at("L", [P, 3, SEQ], 72)
        PT = at("PT", [P, 2, SEQ], 84)
        dtok = at("dtok", [P, BANK], 92)
        M0 = at("M0", [P, 2, D], 186)
        MS = at("MS", [P, 2, KT, N_MEM], 168, F32R)
        sqk = at("sqk", [P, 4, N_MEM], 186)
        kX = at("kX", [P, 4, N_MEM], 194)
        vX = at("vX", [P, 4, N_MEM], 198)
        vXt = at("vXt", [P, 2, BANK], 202)
        qX = at("qX", [P, 4, SEQ], 168)
        sqx = at("sqx", [P, 4, SEQ], 56)
        Pb = at("Pb", [P, 2, 4 * N_MEM], 72)
        PTx = at("PTx", [P, 4, 2, BANK], 104)
        AS = at("AS", [P, 2, 2, SEQ], 168, F32R)
        sil = at("sil", [P, SEQ], 184)
        prod = at("prod", [P, SEQ], 188)

        psf = ps[:, :, :].rearrange("p b c -> p (b c)")

        w_in0, w_out0, w_xq0, w_xkv0, w_xo0, w_gu0, w_dn0 = (
            a[0] for a in (w_in, w_out, w_xq, w_xkv, w_xo, w_gu, w_down))

        def cols_of(w, c, n=P):
            return w[:, bass.ds(c, n)].rearrange("(k p) c -> p k c", p=P)

        units = ["small"]
        units += [cols_of(w_in0, C_IQ + a * P) for a in range(8)]
        N_QKV = len(units)
        units += [cols_of(w_in0, C_QKV + a * P) for a in range(12)]
        N_Z = len(units)
        units += [cols_of(w_in0, C_Z + a * P) for a in range(4)]
        units += [cols_of(w_in0, C_DQ + a * P) for a in range(12)]
        N_OUT = len(units)
        units += [w_out0[k * P:(k + 1) * P, :] for k in range(8)]
        N_KV = len(units)
        units += [cols_of(w_xkv0, a * P) for a in range(8)]
        N_XQ = len(units)
        units += [cols_of(w_xq0, a * P) for a in range(4)]
        N_XO = len(units)
        units += [w_xo0[k * P:(k + 1) * P, :] for k in range(4)]
        N_FF = len(units)
        PER = 6
        assert PER % RING == 0

        ups, pairs, freed = {}, {}, []
        for n in range(N_FF):
            if N_OUT <= n < N_KV or n >= N_XO:
                pairs.setdefault(n - (n - N_OUT) % 2 if n < N_KV else n - (n - N_XO) % 2, len(pairs))
                freed.append(("pair", len(pairs)))
            else:
                ups[n] = len(ups)
                freed.append(("up", len(ups)))
        UPS_FF, PAIRS_FF = len(ups), len(pairs)
        landed = [sem(f"w_landed{i}") for i in range(RING)]
        landed_at, have = [], [0] * RING
        for n in range(N_FF):
            have[n % RING] += 32 if n == 0 else 16
            landed_at.append(have[n % RING])
        w_hi = sem("w_hi")
        w_split = sem("w_split")
        unit_done = sem("unit_done")
        down_out = sem("down_out")
        down_add = sem("down_add")
        up_freed = sem("up_freed")
        consts = sem("consts")
        x_in = [sem(f"x_in{i}") for i in range(4)]
        row_in = sem("row_in")
        gB_in = sem("gB_in")
        met = sem("met")
        meetings = [0, 0, 0]

        def meet(i, eng):
            meetings[i] += 1
            eng.drain().then_inc(met, 1)
            eng.wait_ge(met, 3 * meetings[i])

        a_chain, d_chain, p_chain = sem("act_chain"), sem("dve_chain"), sem("pool_chain")
        linked = {"a": 0, "d": 0, "p": 0}

        def link(key, eng, chain, ins):
            linked[key] += 1
            ins.then_inc(chain, 1)
            eng.wait_ge(chain, linked[key])

        class Norm:
            def __init__(self, tag, X, n, dst, ready):
                self.X, self.n, self.dst, self.ready = X, n, dst, ready
                self.ss, self.sd, self.rs, self.xn, self.tr, self.hi, self.lo = (
                    sem(f"{tag}_{x}") for x in ("ss", "sd", "rs", "xn", "tr", "hi", "lo"))

        def dst_of(m, part, t, j):
            return m.dst[:, part, 4 * j:4 * j + 4, t * P:(t + 1) * P]

        def blocks(bank):
            return ps[:, bank, :].rearrange("p (k c) -> p k c", c=P)

        def norm_act(act, m):
            def evac(t):
                for j in range(2):
                    act.wait_ge(m.tr, 2 * t + j + 1)
                    act.activation(dst_of(m, 0, t, j), blocks(2 * (t % 4) + j), ACT.Copy).then_inc(m.hi, 1)
            for t in range(m.n):
                m.ready(act, t)
                if t >= 2:
                    act.wait_ge(m.ss, t - 1)
                act.activation(junk[:, t % 2, :], m.X[:, t, :], ACT.Square,
                               accum_out=ss[:, t:t + 1]).then_inc(m.ss, 1)
                act.wait_ge(m.ss, t + 1)
                act.activation(sd[:, t:t + 1], ss[:, t:t + 1], ACT.Sqrt, bias=eps_t[:, 0:1],
                               scale=1.0 / D).then_inc(m.sd, 1)
                if t:
                    evac(t - 1)
            evac(m.n - 1)

        def norm_dve(dve, m, g_count):
            def lo(t):
                for j in range(2):
                    dve.wait_ge(m.hi, 2 * t + j + 1)
                    dve.tensor_tensor(dst_of(m, 1, t, j), blocks(2 * (t % 4) + j),
                                      dst_of(m, 0, t, j).bitcast(F32), ALU.subtract).then_inc(m.lo, 1)
            dve.wait_ge(gB_in, 16 * g_count)
            for t in range(m.n):
                dve.wait_ge(m.sd, t + 1)
                dve.reciprocal(rs[:, t:t + 1], sd[:, t:t + 1]).then_inc(m.rs, 1)
                dve.wait_ge(m.rs, t + 1)
                if t >= 2:
                    dve.wait_ge(m.tr, 2 * (t - 1))
                dve.scalar_tensor_tensor(xn[:, t % 2, :], m.X[:, t, :], rs[:, t:t + 1], gB[:, :],
                                         ALU.mult, ALU.mult).then_inc(m.xn, 1)
                if t:
                    lo(t - 1)
            lo(m.n - 1)

        def norm_pe(pe, m):
            for t in range(m.n):
                pe.wait_ge(m.xn, t + 1)
                if t >= 4:
                    pe.wait_ge(m.lo, 2 * (t - 3))
                for j in range(2):
                    for k in range(4):
                        mm = pe.transpose(ps[:, 2 * (t % 4) + j, k * P:(k + 1) * P],
                                          xn[:, t % 2, (4 * j + k) * P:(4 * j + k + 1) * P], ident[:, :])
                    mm.then_inc(m.tr, 1)

        def up_pe(pe, n, src, width, ncol=P, between=None):
            m = ups[n]
            pe.wait_ge(w_split, n + 1)
            if m >= 2:
                pe.wait_ge(up_freed, m - 1)
            for half, (c, w) in enumerate(chunks(width)):
                acc = ps[0:ncol, 2 * (m % 2) + half, 0:w]
                for k in range(KT):
                    hi, lo = (WS[:, n % RING, s, k * ncol:(k + 1) * ncol] for s in (0, 1))
                    pe.matmul(acc, lo, src[:, 0, k, c:c + w], start=(k == 0), stop=False)
                    pe.matmul(acc, hi, src[:, 1, k, c:c + w], start=False, stop=False)
                    mm = pe.matmul(acc, hi, src[:, 0, k, c:c + w], start=False, stop=(k == KT - 1))
                    if between and half * KT + k + 1 < HALVES * KT:
                        between(half * KT + k)
            mm.then_inc(unit_done, 1)

        def up_bank(n, half):
            return ps[:, 2 * (ups[n] % 2) + half, :]

        def down_pe(pe, slots, split, blk, lhs, ready):
            for r in range(4):
                for s in range(2):
                    if r == 0:
                        pe.wait_ge(w_split, split - 1 + s)
                        ready(s)
                    for q in range(4):
                        t, h = (4 * r + q) // 2, q % 2
                        if s == 0 and (r or blk is not None):
                            pe.wait_ge(down_add, (0 if blk is None else blk) + 4 * r + q - 3)
                        whi, wlo = (WS[:, slots[s], a, h * BANK:(h + 1) * BANK] for a in (0, 1))
                        xhi, xlo = lhs(s, t)
                        acc = ps[:, 4 + q, :]
                        pe.matmul(acc, xlo, whi, start=(s == 0), stop=False)
                        pe.matmul(acc, xhi, wlo, start=False, stop=False)
                        mm = pe.matmul(acc, xhi, whi, start=False, stop=(s == 1))
                        if s == 1:
                            mm.then_inc(down_out, 1)

        def down_dve(dve, blk, first=False):
            for o in range(16):
                t, h = o // 2, o % 2
                dve.wait_ge(down_out, blk + o + 1)
                if not first:
                    dve.wait_ge(down_add, blk + o - 15)
                xs = X[:, t, h * BANK:(h + 1) * BANK]
                dve.tensor_tensor(xs, xs, ps[:, 4 + o % 4, :], ALU.add).then_inc(down_add, 1)

        small_ev = sem("small_evac")
        wba_tr, wba_ev = sem("wba_tr"), sem("wba_ev")
        qi_hi = sem("qi_hi")
        qi_lo = sem("qi_lo")
        dots_out, relu_out, acc_out = sem("dots_out"), sem("relu_out"), sem("score_acc")
        dots_used = sem("dots_used")
        entries = [(a, j, t, c, w) for a in range(8) for j in range(2) for t in range(TT)
                   for c, w in chunks((t + 1) * P)]
        PER_A = len(entries) // 8
        PER_J = PER_A // 2
        raw_in, conv_ev, silu_ev = sem("raw_in"), sem("conv"), sem("silu")
        spilled = [sem("spilled0"), sem("spilled1")]
        topk = sem("topk")
        bias_ev = sem("logit_bias")
        cols_ev = sem("cols_tr")
        cols_sb = sem("cols_sb")

        norm1 = Norm("n1", X, TT, HS, lambda e, t: e.wait_ge(x_in[t // 2], 16))
        norm_m = Norm("nm", M0, 2, MS, lambda e, t: e.wait_ge(m_in, 16))
        m_in = sem("mem_in")
        norm2 = Norm("n2", X, TT, HS, lambda e, t: e.wait_ge(down_add, 16 * 3 + 2 * t + 2))
        norm3 = Norm("n3", X, TT, HS, lambda e, t: e.wait_ge(down_add, 16 * 5 + 2 * t + 2))

        LV = range(1, 6)
        g0p = steps("g0_pe", ["stat", "sums"] + [f"bc{e}" for e in range(16)])
        g0a = steps("g0_act", ["beta", "abs", "exp", "ln", "ea"] + [f"sq{u}" for u in range(8)]
                    + ["sd", "ed", "erem", "last"])
        g0d = steps("g0_dve", ["z", "max", "sp", "g", "rs", "rq", "nbed"] + [f"n{e}" for e in range(16)])
        gp = steps("gdn_pe", ["k0", "k1", "v0", "v1", "GQ", "diff", "db0", "db1", "x0"]
                   + [f"{x}{s}" for s in LV for x in (("y", "zt", "z") if s < 5 else ("y", "zt"))] + ["w0", "w1"])
        gd = steps("gdn_dve", ["nk0", "kd0", "nk1", "kd1", "vb0", "vb1", "A1", "Q1", "qd0", "qd1", "TT0"]
                   + [f"{x}{s}" for s in LV for x in (("TT", "T") if s < 5 else ("TT",))])
        ga = steps("gdn_act", ["gA", "gQ", "e0", "e1"] + [f"y{s}" for s in LV] + ["w0", "w1"])
        gl = steps("gdn_pool", ["gM", "gU", "bM", "A", "Q", "X0", "T0"] + [f"X{s}" for s in LV])
        sp_, sd_ = steps("scan_pe", ["v", "s", "o"]), steps("scan_dve", ["S"])
        sa_, sl_ = steps("scan_act", ["vn", "ot"]), steps("scan_pool", ["Sl"])
        tp = steps("gpost_pe", [f"tr{i}" for i in range(TT)])
        T_ON = 6
        td = steps("gpost_dve", ["r0"] + [f"on0{h}" for h in range(4)] + ["r1"] + [f"on1{h}" for h in range(4)]
                   + [f"y{i}" for i in range(TT)])
        ta = steps("gpost_act", [f"q{t}" for t in range(T_ON)] + ["sd0"] + [f"q{t}" for t in range(T_ON, TT)] + ["sd1"])
        z_in = sem("z_in")

        qk_in = [sem(f"qk_in{i}") for i in range(3)]
        d0p = steps("d0_pe", [f"st{e}" for e in range(16)] + [f"bc{e}" for e in range(16)])
        d0a = steps("d0_act", [f"sq{e}" for e in range(16)] + ["sd"])
        d0d = steps("d0_dve", ["rs"] + [f"n{e}" for e in range(16)])
        q_odd, q_pad = sem("q_odd"), sem("q_pad")
        v_tr, v_ev = sem("v_tr"), sem("v_ev")
        lg, Lw, mx, ex, ptr, pte, pvs = (sem("dsa_" + x) for x in ("lg", "L", "max", "exp", "ptr", "pt", "pv"))
        heads = [(t, h) for t in range(TT) for h in range(SH)]
        ptc = [0]
        for t, h in heads:
            ptc.append(ptc[-1] + len(chunks((t + 1) * P)))
        drp, dnd, dtr, dyb = sem("dsa_r"), sem("dsa_norm"), sem("dsa_tr"), sem("dsa_y")
        hs_hi, hs_lo = sem("hs_hi"), sem("hs_lo")
        xr_in = sem("x_again")

        xkp = steps("xk_pe", ["stat", "bc0", "bc1", "v0", "v1"])
        xka = steps("xk_act", ["sq", "sd", "v0", "v1"])
        xkd = steps("xk_dve", ["rs", "n0", "n1"])
        x0p = steps("xq_pe", ["stat"] + [f"bc{e}" for e in range(8)])
        x0a = steps("xq_act", [f"sq{u}" for u in range(4)] + ["sd"])
        x0d = steps("xq_dve", ["rs"] + [f"n{e}" for e in range(8)])
        xlg, xmx, xex, xr, xpn, xptr, xpte = (sem("xa_" + x) for x in ("lg", "max", "exp", "r", "pn", "ptr", "pt"))
        xo_, xohi, xolo = sem("xa_o"), sem("xa_ohi"), sem("xa_olo")

        f_sil, f_prod, f_hi, f_lo = sem("ff_silu"), sem("ff_prod"), sem("ff_hi"), sem("ff_lo")
        out_sem = sem("out_stored")

        def bc(ap, shape):
            return ap.to_broadcast(shape)

        def unit_b(t, c0, n):
            return t[:, c0:c0 + n].unsqueeze(2)

        PREP = ["in", "gq", "mask", "decay", "x0"] + [f"{x}{s}" for s in LV for x in "yz"] + ["w"]

        def half_unit(e):
            u, half = e // 2, e % 2
            return u, (kD if u < 4 else qD)[:, u % 4, half * BANK:(half + 1) * BANK], half

        DSA_PARTS = {0: ("top", 0, 0), 1: ("top", 0, 0), 2: ("on", 0, 0), 3: ("sq", 0, 8), 4: ("sq", 8, 16),
                     5: ("sd", 0, 0), 6: ("bc", 0, 8), 7: ("bc", 8, 16)}

        def gdn_order(prep, scan_v, scan_s, dsa):
            for part in PREP:
                prep(0, part)
            for c in range(SEQ // CHUNK):
                parts = PREP[4 * (c % 4):4 * (c % 4) + 4] if c // 4 < 3 else []
                scan_v(c)
                for part in parts[:2]:
                    prep(c // 4 + 1, part)
                if 2 * (c - 12) in DSA_PARTS:
                    dsa(*DSA_PARTS[2 * (c - 12)])
                scan_s(c)
                for part in parts[2:]:
                    prep(c // 4 + 1, part)
                if 2 * (c - 12) + 1 in DSA_PARTS:
                    dsa(*DSA_PARTS[2 * (c - 12) + 1])

        MEET_MIX, MEET_DSA = 1, 5
        block = ctx.enter_context(nc.Block())

        @block.sync
        def _(sp):
            def load(n, view=None, split_at=None):
                if n >= RING:
                    sp.wait_ge(w_split, n + 1 - RING)
                slot = n % RING
                if n == 0:
                    for c, w, d in ((C_IK, 80, 0), (C_B, 8, 80)):
                        sp.dma_start(WR[:, 0, 0:KT * N_SMALL].rearrange("p (k c) -> p k c", c=N_SMALL)[:, :, d:d + w],
                                     cols_of(w_in0, c, w)).then_inc(landed[0], 16)
                elif N_OUT <= n < N_KV or n >= N_XO:
                    sp.dma_start(WR[:, slot, :], units[n]).then_inc(landed[slot], 16)
                else:
                    sp.dma_start(WR[:, slot, :].rearrange("p (k c) -> p k c", c=P), units[n]).then_inc(landed[slot], 16)

            xv = x[0].rearrange("(t p) d -> p t d", p=P)
            for i in range(4):
                sp.dma_start(X[:, 2 * i:2 * i + 2, :], xv[:, 2 * i:2 * i + 2, :]).then_inc(x_in[i], 16)
                if i == 0:
                    sp.dma_start(gB[:, :], g_mix[0:1, :].to_broadcast([P, D])).then_inc(gB_in, 16)
            sp.dma_start(stage[0:48, :], conv_w[0].rearrange("k (u p) -> (k u) p", p=P)).then_inc(row_in, 16)
            for r, g, n in ((48, g_gdn_out, P), (49, g_q_dsa, SD), (50, g_k_dsa, SD), (51, g_xq, P), (52, g_xk, P)):
                for c in range(0, P, n):
                    sp.dma_start(stage[r:r + 1, c:c + n], g[0:1, :]).then_inc(row_in, 16)
            sp.dma_start(dtB[:, :], dt_bias[0:1, :].to_broadcast([P, 4])).then_inc(row_in, 16)
            sp.dma_start(alB[:, :], a_log[0:1, :].to_broadcast([P, 4])).then_inc(row_in, 16)
            for n in range(N_OUT + 2 * RING):
                load(n)
            for s in spilled:
                sp.wait_ge(s, 16 * 8)
            sp.wait_ge(met, 3 * MEET_MIX)
            back = d_dram.rearrange("(i u) p c -> i p u c", u=4)
            sp.dma_start(vraw[:, :, :], back[2]).then_inc(qk_in[2], 16)
            gp.wait(sp, "w1", 3)
            sp.dma_start(kD[:, :, :], back[1]).then_inc(qk_in[1], 16)
            sp.dma_start(qD[:, :, :], back[0]).then_inc(qk_in[0], 16)
            sp.dma_start(zS[:, :, :], z_dram.rearrange("u p c -> p u c")).then_inc(z_in, 16)
            ta.wait(sp, f"q{TT - 1}")
            sp.dma_start(gB[:, :], g_mem[0:1, :].to_broadcast([P, D])).then_inc(gB_in, 16)
            sp.wait_ge(met, 3 * MEET_DSA)
            sp.dma_start(X[:, :, :], xv).then_inc(xr_in, 16)
            sp.wait_ge(hs_lo, 8)
            sp.dma_start(M0[:, :, :], mem[0].rearrange("(t p) d -> p t d", p=P)).then_inc(m_in, 16)
            for n in range(N_OUT + 2 * RING, N_KV + 2 * RING):
                load(n)
            sp.wait_ge(norm_m.xn, 2)
            sp.dma_start(gB[:, :], g_xattn[0:1, :].to_broadcast([P, D])).then_inc(gB_in, 16)
            for n in range(N_KV + 2 * RING, N_XQ + 2 * RING):
                load(n)
            sp.wait_ge(norm2.xn, TT)
            sp.dma_start(gB[:, :], g_ffn[0:1, :].to_broadcast([P, D])).then_inc(gB_in, 16)
            for n in range(N_XQ + 2 * RING, N_FF):
                load(n)
            with sp.Fori(0, FFG) as g:
                for j in range(PER):
                    slot = (N_FF + j) % RING
                    sp.wait_ge(w_split, g * PER + (N_FF + j + 1 - RING))
                    if j < 4:
                        c = g * 256 + (j // 2) * P + (j % 2) * D_FF
                        sp.dma_start(WR[:, slot, :].rearrange("p (k c) -> p k c", c=P),
                                     cols_of(w_gu0, c)).then_inc(landed[slot], 16)
                    else:
                        sp.dma_start(WR[:, slot, :], w_dn0[bass.ds(g * 256 + (j - 4) * P, P), :]).then_inc(landed[slot], 16)
            for t in range(TT):
                sp.wait_ge(down_add, 16 * (PAIRS_FF + FFG - 1) + 2 * t + 2)
                sp.dma_start(out[0, t * P:(t + 1) * P, :], X[:, t, :]).then_inc(out_sem, 16)
            sp.wait_ge(out_sem, 16 * TT)

        @block.gpsimd
        def _(pool):
            def step(ins):
                link("p", pool, p_chain, ins)

            def select(tile, pattern, base_, cm, op=ALU.is_ge, fill=0.0):
                step(pool.affine_select(out=tile, in_=tile, pattern=pattern, compare_op=op, fill=fill,
                                        base=base_, channel_multiplier=cm))

            pool.memset(eps_t[:, :], EPS)
            step(pool.memset(ident[:, :], 0.0))
            select(ident[:, :], [[-1, P]], 0, 1, ALU.not_equal, 1.0)
            pool.memset(ones1[:, :], 1.0)
            pool.memset(zero1[:, :], 0.0)
            pool.memset(blk2[:, :], 0.0)
            pool.memset(half_ones[:, :], 0.0)
            pool.memset(Lev[:, :], 0.0)
            pool.memset(Mblk[:, :], 1.0)
            step(pool.memset(Ublk[:, :], 1.0))
            pool.drain().then_inc(consts, 1)

            def split(n_split, slot, land, free, cols):
                pool.wait_ge(landed[slot], land)
                if free is not None:
                    pool.wait_ge(free[0], free[1])
                hi, lo, w = WS[:, slot, 0, 0:cols], WS[:, slot, 1, 0:cols], WR[:, slot, 0:cols]
                pool.tensor_tensor(hi, w, bc(zero1[:, 0:1], [P, cols]), ALU.add).then_inc(w_hi, 1)
                pool.wait_ge(w_hi, n_split + 1)
                pool.tensor_tensor(lo, w, hi.bitcast(F32), ALU.subtract).then_inc(w_split, 1)

            def split_of(n):
                free = None
                if n >= RING:
                    kind, count = freed[n - RING]
                    free = (unit_done, count) if kind == "up" else (down_out, 16 * count)
                split(n, n % RING, landed_at[n], free, KT * N_SMALL if n == 0 else 1024)

            for n in range(RING):
                split_of(n)
            select(Ublk[:, :], [[1, P]], 0, -1)
            step(pool.memset(Ublk[0:CHUNK, CHUNK:P], 0.0))
            select(Mblk[:, :], [[-1, P]], -1, 1)
            step(pool.memset(Mblk[CHUNK:P, 0:CHUNK], 0.0))
            pool.memset(half_ones[0:CHUNK, 0:P], 1.0)
            pool.memset(half_ones[CHUNK:P, P:2 * P], 1.0)
            pool.memset(blk2[0:CHUNK, 0:1], 1.0)
            pool.memset(blk2[CHUNK:P, 1:2], 1.0)
            for r in (0, CHUNK):
                rows = slice(r, r + CHUNK)
                for dst, src in ((Us, Ublk), (Ms, Mblk), (I64, ident)):
                    pool.tensor_copy(dst[rows, :], src[rows, r:r + CHUNK])
                for s in range(6):
                    w = 1 << s
                    lev = Lev[rows, s * CHUNK:(s + 1) * CHUNK].rearrange("p (b c) -> p b c", c=2 * w)[:, :, 0:w]
                    nb = CHUNK // (2 * w)
                    step(pool.memset(lev, 1.0))
                    select(lev, [[-2 * w, nb], [0, w]], -w, 1)
                    select(lev, [[2 * w, nb], [0, w]], 2 * w - 1, -1)
            step(pool.iota(negdist[:, :], pattern=[[-1, SEQ]], base=SEQ - P, channel_multiplier=1,
                           allow_small_or_imprecise_dtypes=True))
            pool.drain().then_inc(consts, 1)
            for n in range(RING, N_OUT + RING):
                split_of(n)

            def v8(ap):
                return ap.rearrange("p (u c) -> p u c", c=CHUNK)

            def mask_of(m):
                return bc(m.unsqueeze(1), [P, 8, CHUNK])

            def prep(b, part):
                B = b % 2
                if part == "in":
                    if b:
                        gp.wait(pool, "w1", b - 1)
                    else:
                        g0d.wait(pool, "g")
                        g0a.wait(pool, "beta")
                    for dst, by, m, name in ((gMU[:, 0, :], gdec, Ms, "gM"), (gMU[:, 1, :], gdec, Us, "gU"),
                                             (Xm[:, :], beta, Ms, "bM")):
                        if b == 0 and name == "gM":
                            pool.wait_ge(met, 3 * 2)
                        gl.mark(pool.tensor_tensor(v8(dst), bc(by[:, 8 * b:8 * b + 8].unsqueeze(2), [P, 8, CHUNK]),
                                                   mask_of(m[:, :]), ALU.mult), name, b)
                elif part == "mask":
                    gd.wait(pool, "A1", b)
                    gl.wait(pool, "bM", b)
                    gl.mark(pool.tensor_tensor(Am[:, :], Am[:, :], Xm[:, :], ALU.mult), "A", b)
                    gd.wait(pool, "Q1", b)
                    gl.mark(pool.tensor_tensor(v8(QKm[:, B, :]), v8(QKm[:, B, :]), mask_of(Us[:, :]), ALU.mult), "Q", b)
                    gl.wait(pool, "A", b)
                    gl.mark(pool.tensor_tensor(v8(Xm[:, :]), v8(Am[:, :]), mask_of(Lev[:, 0:CHUNK]), ALU.mult), "X0", b)
                    gl.wait(pool, "X0", b)
                    gl.mark(pool.tensor_tensor(v8(Tm[:, :]), mask_of(I64[:, :]), v8(Xm[:, :]), ALU.subtract), "T0", b)
                elif part[0] == "z" or part == "decay":
                    s = 1 if part == "decay" else int(part[1]) + 1
                    if s > 5:
                        return
                    if s <= 2:
                        gd.wait(pool, "qd1", b)
                    else:
                        gp.wait(pool, f"y{s - 2}", b)
                    gl.mark(pool.tensor_tensor(v8(gam[:, s % 2, :]), v8(Am[:, :]),
                                               mask_of(Lev[:, s * CHUNK:(s + 1) * CHUNK]), ALU.mult), f"X{s}", b)

            def scan_s(c):
                if c + 1 == SEQ // CHUNK:
                    return
                l0 = 32 * ((c + 1) % 2) + 4 * ((c + 1) // 2)
                sd_.wait(pool, "S", c)
                sl_.mark(pool.tensor_tensor(Sl[:, :].rearrange("p (h c) -> p h c", c=P),
                                            S[:, (c + 1) % 2, :].rearrange("p (h c) -> p h c", c=P),
                                            bc(lastb[:, l0:l0 + 4].unsqueeze(2), [P, 4, P]), ALU.mult), "Sl", c)

            gdn_order(prep, lambda c: None, scan_s, lambda part, e0, e1: None)
            tp.wait(pool, f"tr{TT - 1}")
            pool.memset(qO[0:SD, :, :], 0.0).then_inc(q_pad, 1)
            pool.wait_ge(q_odd, 1)
            pool.memset(qD[SD:P, :, :], 0.0).then_inc(q_pad, 1)
            for n in range(N_OUT + RING, N_FF):
                split_of(n)
            land0 = [have[i] for i in range(RING)]
            with pool.Fori(0, FFG) as g:
                for j in range(PER):
                    slot = (N_FF + j) % RING
                    if j == 0:
                        pool.wait_ge(down_out, g * 16 + 16 * (PAIRS_FF - 1))
                        free = (unit_done, g * 4 + UPS_FF)
                    elif j < RING:
                        free = (down_out, g * 16 + 16 * PAIRS_FF)
                    else:
                        free = (unit_done, g * 4 + (UPS_FF + j - RING + 1))
                    split(g * PER + (N_FF + j), slot, g * 32 + (have[slot] + 16 * (1 + j // RING)), free, 1024)

        def tap(u, k):
            return cols_t[:, k * 12 + u:k * 12 + u + 1]

        gO, gQ, gK, gXQ, gXK = (cols_t[:, c:c + 1] for c in (48, 53, 50, 54, 52))

        def wcol(c0, n):
            return wba[:, :].rearrange("p (t c) -> p t c", c=24)[:, :, c0:c0 + n]

        def th(t, c0=0):
            return t[:, c0:c0 + 32].rearrange("p (t h) -> p t h", h=4)

        def rows_of(c):
            r0 = CHUNK * (c % 2)
            return c // 4, slice(r0, r0 + CHUNK), r0, 4 * ((c % 4) // 2)

        @block.tensor
        def _(pe):
            pe.wait_ge(consts, 1)
            norm_pe(pe, norm1)
            pe.wait_ge(norm1.lo, 2 * TT)
            up_pe(pe, 0, HS, SEQ, N_SMALL)
            up_pe(pe, 1, HS, SEQ)
            pe.wait_ge(small_ev, 2)
            for t in range(TT):
                mm = pe.transpose(ps[:, 4, t * 24:(t + 1) * 24], wT[0:24, t * P:(t + 1) * P], ident[0:24, 0:24])
            mm.then_inc(wba_tr, 1)
            pe.wait_ge(row_in, 16 * 10)
            pe.transpose(ps[:, 5, 0:53], stage[0:53, :], ident[0:53, 0:53]).then_inc(cols_ev, 1)
            up_pe(pe, 2, HS, SEQ)
            pe.wait_ge(wba_ev, 2)
            pe.wait_ge(cols_sb, 1)
            for a in range(8):
                pe.wait_ge(qi_lo, a + 1)

                def dots(i):
                    e = a * PER_A + i
                    _, j, t, c, w = entries[e]
                    if e >= 4:
                        pe.wait_ge(relu_out, e - 3)
                    for part in range(2):
                        mm = pe.matmul(ps[:, 4 + e % 4, 0:w], qI[:, a % 2, j, t * P:(t + 1) * P],
                                       kI[:, part, c:c + w], start=(part == 0), stop=(part == 1))
                    mm.then_inc(dots_out, 1)

                steps_k = HALVES * KT - 1

                def between(i):
                    for j in range(i * PER_A // steps_k, (i + 1) * PER_A // steps_k):
                        dots(j)
                up_pe(pe, a + 3, HS, SEQ, between=between)
            for n in range(11, N_OUT):
                up_pe(pe, n, HS, SEQ)
            meet(0, pe)

            for u in range(8):
                g0a.wait(pe, f"sq{u}")
                for t in range(TT):
                    mm = pe.matmul(ps[:, 4, u * TT + t:u * TT + t + 1], sqg[:, u, t * P:(t + 1) * P],
                                   ones1[:, 0:1], start=True, stop=True)
            g0p.mark(mm, "stat")
            pe.wait_ge(consts, 2)
            g0d.wait(pe, "g")
            for i, lhs in enumerate((Ublk[:, :], Mblk[:, :], half_ones[:, 0:P], half_ones[:, P:2 * P])):
                mm = pe.matmul(ps[:, 5, 32 * i:32 * i + 32], lhs, gdec[:, :], start=True, stop=True)
            g0p.mark(mm, "sums")
            g0d.wait(pe, "rq")
            for e in range(16):
                u, half = e // 2, e % 2
                if e >= 4:
                    g0d.wait(pe, f"n{e - 4}")
                for q in range(4):
                    col = u * TT + half * 4 + q
                    mm = pe.matmul(ps[:, e % 4, q * P:(q + 1) * P], bc(rs[:, col:col + 1], [P, P]), ident[:, :],
                                   start=True, stop=True)
                g0p.mark(mm, f"bc{e}")
            meet(0, pe)

            def per_unit(b, fn):
                for ul in range(8):
                    for par in range(2):
                        r = slice(CHUNK * par, CHUNK * par + CHUNK)
                        mm = fn(ul, par, r)
                return mm

            def prep(b, part):
                B = b % 2
                if part == "in":
                    if b:
                        gd.wait(pe, "TT5", b - 1)
                        ga.wait(pe, "w1", b - 1)
                    for src, b0 in ((4, 0), (8, 2)):
                        for tl in range(2):
                            tok = slice((2 * b + tl) * P, (2 * b + tl + 1) * P)
                            for h in range(4):
                                mm = pe.transpose(ps[:, b0 + tl, h * P:(h + 1) * P], QKV[:, src + h, tok], ident[:, :])
                            gp.mark(mm, ("k" if src == 4 else "v") + str(tl), b)
                elif part == "gq":
                    gd.wait(pe, "kd1", b)

                    def gq(bank, src):
                        def fn(ul, par, r):
                            c0 = (2 * b + ul // 4) * P + par * CHUNK
                            c = slice(c0, c0 + CHUNK)
                            return pe.matmul(ps[r, bank, ul * CHUNK:(ul + 1) * CHUNK], QKV[:, 4 + ul % 4, c],
                                             QKV[:, src + ul % 4, c], start=True, stop=True)
                        return fn
                    per_unit(b, gq(0, 4))
                    gp.mark(per_unit(b, gq(1, 0)), "GQ", b)
                    gd.wait(pe, "vb1", b)
                    gl.wait(pe, "gU", b)
                    pe.matmul(ps[:, 2, :], Ublk[:, :], gMU[:, 0, :], start=True, stop=True)
                    gp.mark(pe.matmul(ps[:, 3, :], Mblk[:, :], gMU[:, 1, :], start=True, stop=True), "diff", b)
                elif part == "decay":
                    ga.wait(pe, "gQ", b)
                    for j in range(2):
                        for q in range(4):
                            col = 8 * b + 4 * j + q
                            mm = pe.matmul(ps[:, 2 + j, q * P:(q + 1) * P], bc(gdec[:, col:col + 1], [P, P]),
                                           Ublk[:, :], start=True, stop=True)
                        gp.mark(mm, f"db{j}", b)
                elif part == "x0":
                    gl.wait(pe, "X0", b)
                    gp.mark(per_unit(b, lambda ul, par, r: pe.matmul(
                        ps[r, 0, ul * CHUNK:(ul + 1) * CHUNK], Xm[r, ul * CHUNK:(ul + 1) * CHUNK], I64[r, :],
                        start=True, stop=True)), "x0", b)
                elif part[0] in "yz":
                    s = int(part[1])

                    def tri(bank, lhs, rhs):
                        return per_unit(b, lambda ul, par, r: pe.matmul(
                            ps[r, bank, ul * CHUNK:(ul + 1) * CHUNK], lhs[r, ul * CHUNK:(ul + 1) * CHUNK],
                            rhs[r, ul * CHUNK:(ul + 1) * CHUNK], start=True, stop=True))
                    if part[0] == "y":
                        gl.wait(pe, f"X{s}", b)
                        gd.wait(pe, f"TT{s - 1}", b)
                        gp.mark(tri(0, gam[:, s % 2, :], TTm[:, B, :]), f"y{s}", b)
                    else:
                        ga.wait(pe, f"y{s}", b)
                        if s > 1:
                            gd.wait(pe, f"T{s - 1}", b)
                        gp.mark(tri(1, Tm[:, :], Ym[:, :]), f"zt{s}", b)
                        if s < 5:
                            gp.mark(tri(2, Ym[:, :], Tm[:, :]), f"z{s}", b)
                elif part == "w":
                    gd.wait(pe, "TT5", b)
                    for ul in range(8):
                        for par in range(2):
                            r = slice(CHUNK * par, CHUNK * par + CHUNK)
                            c = slice(ul * CHUNK, (ul + 1) * CHUNK)
                            mm = pe.matmul(ps[:, 2 + par, c], nkbd[r, ul * P:(ul + 1) * P], TTm[r, B, c],
                                           start=True, stop=True)
                            if ul == 7:
                                gp.mark(mm, f"w{par}", b)

            def scan_v(c):
                b, r, r0, u0 = rows_of(c)
                B = b % 2
                if c % 4 == 0:
                    ga.wait(pe, "w1", b)
                    gd.wait(pe, "TT5", b)
                    gl.wait(pe, "X5", b)
                if c:
                    sa_.wait(pe, "vn", c - 1)
                for h in range(4):
                    mm = pe.matmul(ps[r, 4, h * P:(h + 1) * P], TTm[r, B, (u0 + h) * CHUNK:(u0 + h + 1) * CHUNK],
                                   vb[r, B, (u0 + h) * P:(u0 + h + 1) * P], start=(h == 0), stop=(c == 0 and h == 3),
                                   skip_group_check=True)
                if c:
                    sd_.wait(pe, "S", c - 1)
                    for h in range(4):
                        w0 = 8 * r0 + (u0 + h) * CHUNK
                        mm = pe.matmul(ps[r, 4, h * P:(h + 1) * P], wTt[:, B, w0:w0 + CHUNK],
                                       S[:, c % 2, h * P:(h + 1) * P], start=False, stop=(h == 3), skip_group_check=True)
                sp_.mark(mm, "v", c)
                if c:
                    sa_.wait(pe, "ot", c - 1)
                    for h in range(4):
                        w0 = (u0 + h) * P + r0
                        pe.matmul(ps[r, 5, h * P:(h + 1) * P], qdec[:, B, w0:w0 + CHUNK],
                                  S[:, c % 2, h * P:(h + 1) * P], start=(h == 0), stop=False, skip_group_check=True)

            def scan_s(c):
                b, r, r0, u0 = rows_of(c)
                B = b % 2
                sa_.wait(pe, "vn", c)
                for h in range(4):
                    mm = pe.matmul(ps[:, 6, h * P:(h + 1) * P], kdec[r, B, (u0 + h) * P:(u0 + h + 1) * P],
                                   vn[r, h * P:(h + 1) * P], start=True, stop=True)
                sp_.mark(mm, "s", c)
                for h in range(4):
                    mm = pe.matmul(ps[r, 5, h * P:(h + 1) * P], QKm[r, B, (u0 + h) * CHUNK:(u0 + h + 1) * CHUNK],
                                   vn[r, h * P:(h + 1) * P], start=(c == 0 and h == 0), stop=(h == 3),
                                   skip_group_check=True)
                sp_.mark(mm, "o", c)

            def dsa(part, e0, e1):
                for e in range(e0, e1):
                    u, src, half = half_unit(e)
                    if part == "sq":
                        d0a.wait(pe, f"sq{e}")
                        for q in range(4):
                            c = 2 * (u * TT + half * 4 + q)
                            mm = pe.matmul(ps[:, 7, c:c + 2], sqh[:, e % 2, q * P:(q + 1) * P], blk2[:, :],
                                           start=True, stop=True)
                        d0p.mark(mm, f"st{e}")
                    elif part == "bc":
                        d0d.wait(pe, "rs")
                        if e >= 4:
                            d0d.wait(pe, f"n{e - 4}")
                        for q in range(4):
                            c = 2 * (u * TT + half * 4 + q)
                            for j in range(2):
                                mm = pe.matmul(ps[SD * j:SD * (j + 1), e % 4, q * P:(q + 1) * P],
                                               bc(rs[:, c + j:c + j + 1], [P, SD]), ident[:, :], start=True, stop=True)
                        d0p.mark(mm, f"bc{e}")

            gdn_order(prep, scan_v, scan_s, dsa)
            meet(0, pe)
            for t in range(TT):
                if t >= 2:
                    pe.wait_ge(v_ev, t - 1)
                for a in range(4):
                    mm = pe.transpose(ps[:, 6 + t % 2, a * P:(a + 1) * P], vraw[:, a, t * P:(t + 1) * P], ident[:, :])
                mm.then_inc(v_tr, 1)
            for t in range(TT):
                td.wait(pe, "on13")
                if t >= 4:
                    td.wait(pe, f"y{t - 4}")
                for h in range(4):
                    mm = pe.transpose(ps[:, t % 4, h * P:(h + 1) * P], QKV[:, h, t * P:(t + 1) * P], ident[:, :])
                tp.mark(mm, f"tr{t}")
            meet(0, pe)

            def logits(i):
                t, h = heads[i]
                if i >= 2:
                    pe.wait_ge(Lw, i - 1)
                for k, (c, w) in enumerate(chunks((t + 1) * P)):
                    mm = pe.matmul(ps[:, 2 * (i % 2) + k, 0:w], (qO if h % 2 else qD)[:, h // 2, t * P:(t + 1) * P],
                                   kD[:, h // 2, c:c + w], start=True, stop=True)
                mm.then_inc(lg, 1)

            def probs_tr(i):
                t, h = heads[i]
                pe.wait_ge(ex, i + 1)
                for k, (c, w) in enumerate(chunks((t + 1) * P)):
                    if ptc[i] + k >= 2:
                        pe.wait_ge(pte, ptc[i] + k - 1)
                    for q in range(w // P):
                        mm = pe.transpose(ps[:, 4 + (ptc[i] + k) % 2, q * P:(q + 1) * P],
                                          L[:, i % 3, c + q * P:c + (q + 1) * P], ident[:, :])
                    mm.then_inc(ptr, 1)

            def values(i):
                t, h = heads[i]
                pe.wait_ge(pte, ptc[i + 1])
                if h == 0 and t >= 2:
                    pe.wait_ge(dyb, t - 1)
                for s in range(t + 1):
                    mm = pe.matmul(ps[:, 6 + t % 2, h * SD:(h + 1) * SD], PT[:, i % 2, s * P:(s + 1) * P],
                                   vtok[:, s, h * SD:(h + 1) * SD], start=(s == 0), stop=(s == t))
                mm.then_inc(pvs, 1)

            def out_tr(t):
                pe.wait_ge(dnd, t + 1)
                for a in range(4):
                    mm = pe.transpose(ps[:, 6 + t % 2, a * P:(a + 1) * P], dtok[:, a * P:(a + 1) * P], ident[:, :])
                mm.then_inc(dtr, 1)

            N = len(heads)
            pe.wait_ge(q_pad, 2)
            logits(0)
            logits(1)
            for i in range(N):
                probs_tr(i)
                if i + 2 < N:
                    logits(i + 2)
                if i:
                    values(i - 1)
                if heads[i][1] == 4 and heads[i][0]:
                    out_tr(heads[i][0] - 1)
            values(N - 1)
            out_tr(TT - 1)
            meet(0, pe)

            for p in range(4):
                n = N_OUT + 2 * p
                down_pe(pe, [n % RING, (n + 1) % RING], n + 2, 16 * p if p else None,
                        lambda s, t: [HS[:, a, 2 * p + s, t * P:(t + 1) * P] for a in (0, 1)],
                        lambda s: pe.wait_ge(hs_lo, 2 * p + s + 1))
            norm_pe(pe, norm_m)
            pe.wait_ge(norm_m.lo, 4)
            for n in range(N_KV, N_XQ):
                up_pe(pe, n, MS, N_MEM)
            xka.wait(pe, "sq")
            for a in range(4):
                for mt in range(2):
                    mm = pe.matmul(ps[:, 4, 2 * a + mt:2 * a + mt + 1], sqk[:, a, mt * P:(mt + 1) * P],
                                   ones1[:, 0:1], start=True, stop=True)
            xkp.mark(mm, "stat")
            xkd.wait(pe, "rs")
            for j in range(2):
                for q in range(4):
                    col = 4 * j + q
                    mm = pe.matmul(ps[:, 6 + j, q * P:(q + 1) * P], bc(rs[:, col:col + 1], [P, P]), ident[:, :],
                                   start=True, stop=True)
                xkp.mark(mm, f"bc{j}")
            pe.wait_ge(up_freed, ups[N_XQ - 1] + 1)
            for mt in range(2):
                for a in range(4):
                    mm = pe.transpose(ps[:, 4 + mt, a * P:(a + 1) * P], vX[:, a, mt * P:(mt + 1) * P], ident[:, :])
                xkp.mark(mm, f"v{mt}")
            xka.wait(pe, "v1")
            xkd.wait(pe, "n1")
            norm_pe(pe, norm2)
            pe.wait_ge(norm2.lo, 2 * TT)
            for n in range(N_XQ, N_XO):
                up_pe(pe, n, HS, SEQ)
            for u in range(4):
                x0a.wait(pe, f"sq{u}")
                for t in range(TT):
                    mm = pe.matmul(ps[:, 4, u * TT + t:u * TT + t + 1], sqx[:, u, t * P:(t + 1) * P],
                                   ones1[:, 0:1], start=True, stop=True)
            x0p.mark(mm, "stat")
            x0d.wait(pe, "rs")
            for e in range(8):
                u, half = e // 2, e % 2
                if e >= 4:
                    x0d.wait(pe, f"n{e - 4}")
                for q in range(4):
                    col = u * TT + half * 4 + q
                    mm = pe.matmul(ps[:, e % 4, q * P:(q + 1) * P], bc(rs[:, col:col + 1], [P, P]), ident[:, :],
                                   start=True, stop=True)
                x0p.mark(mm, f"bc{e}")
            x0d.wait(pe, "n7")

            def xlogits(t):
                if t >= 2:
                    pe.wait_ge(xex, 4 * (t - 1))
                for h in range(4):
                    b0 = 2 * (t % 2) + h // 2
                    mm = pe.matmul(ps[:, b0, (h % 2) * N_MEM:(h % 2 + 1) * N_MEM], qX[:, h, t * P:(t + 1) * P],
                                   kX[:, h, :], start=True, stop=True)
                mm.then_inc(xlg, 1)

            xlogits(0)
            for t in range(TT):
                if t + 1 < TT:
                    xlogits(t + 1)
                pe.wait_ge(xpn, t + 1)
                for j in range(2):
                    if t:
                        pe.wait_ge(xpte, 2 * (t - 1) + j + 1)
                    for q in range(4):
                        mm = pe.transpose(ps[:, 4 + j, q * P:(q + 1) * P],
                                          Pb[:, t % 2, (4 * j + q) * P:(4 * j + q + 1) * P], ident[:, :])
                    mm.then_inc(xptr, 1)
                if t % 4 == 3:
                    g = t // 4
                    pe.wait_ge(xpte, 2 * t + 2)
                    for h in range(4):
                        i = 4 * g + h
                        if i >= 2:
                            pe.wait_ge(xolo, i - 1)
                        for mt in range(2):
                            mm = pe.matmul(ps[:, 6 + i % 2, :], vXt[:, mt, h * P:(h + 1) * P], PTx[:, h, mt, :],
                                           start=(mt == 0), stop=(mt == 1))
                        mm.then_inc(xo_, 1)
            pe.wait_ge(xpte, 2 * TT)
            pe.wait_ge(xolo, 8)
            for p in range(2):
                n = N_XO + 2 * p
                down_pe(pe, [n % RING, (n + 1) % RING], n + 2, 16 * (4 + p),
                        lambda s, t: [HS[:, a, 2 * p + s, t * P:(t + 1) * P] for a in (0, 1)],
                        lambda s: None)
            norm_pe(pe, norm3)
            pe.wait_ge(norm3.lo, 2 * TT)
            with pe.Fori(0, FFG) as g:
                for j in range(4):
                    slot, b0 = (N_FF + j) % RING, 2 * (j % 2)
                    pe.wait_ge(w_split, g * PER + (N_FF + j + 1))
                    if j % 2 == 0:
                        pe.wait_ge(f_sil, g * 4 + (2 * (j // 2) + 1))
                    else:
                        pe.wait_ge(f_prod, g * 4 + (2 * (j // 2) + 1))
                    for half in range(HALVES):
                        c = slice(half * BANK, (half + 1) * BANK)
                        for k in range(KT):
                            hi, lo = (WS[:, slot, s, k * P:(k + 1) * P] for s in (0, 1))
                            pe.matmul(ps[:, b0 + half, :], lo, HS[:, 0, k, c], start=(k == 0), stop=False)
                            pe.matmul(ps[:, b0 + half, :], hi, HS[:, 1, k, c], start=False, stop=False)
                            mm = pe.matmul(ps[:, b0 + half, :], hi, HS[:, 0, k, c], start=False, stop=(k == KT - 1))
                    mm.then_inc(unit_done, 1)
                down_pe(pe, [(N_FF + 4) % RING, (N_FF + 5) % RING], g * PER + (N_FF + 6), g * 16 + 16 * PAIRS_FF,
                        lambda s, t: [AS[:, s, a, t * P:(t + 1) * P] for a in (0, 1)],
                        lambda s: pe.wait_ge(f_lo, g * 4 + (2 * s + 3)))

        @block.scalar
        def _(act):
            def clink(ins):
                link("a", act, a_chain, ins)

            act.wait_ge(consts, 1)
            norm_act(act, norm1)
            act.wait_ge(unit_done, 1)
            for half in range(HALVES):
                c = slice(half * BANK, (half + 1) * BANK)
                act.activation(wT[0:24, c], ps[64:88, half, :], ACT.Copy)
                for r in (0, SD):
                    ins = act.activation(kI[r:r + SD, 0, c], ps[0:SD, half, :], ACT.Copy)
                ins.then_inc(small_ev, 1)

            def queries(a):
                act.wait_ge(unit_done, a + 2)
                if a >= 2:
                    act.wait_ge(dots_out, (a - 1) * PER_A)
                for half in range(HALVES):
                    for j in range(2):
                        r = slice(SD * j, SD * j + SD)
                        ins = act.activation(qI[r, a % 2, j, half * BANK:(half + 1) * BANK],
                                             up_bank(a + 1, half)[r, :], ACT.Copy)
                    ins.then_inc(qi_hi, 1)

            queries(0)
            act.wait_ge(wba_tr, 1)
            w4 = ps[:, 4, 0:TT * 24].rearrange("p (t c) -> p t c", c=24)
            act.activation(wcol(0, IH), w4[:, :, 0:IH], ACT.Copy, scale=IH ** -0.5 * SD ** -0.5).then_inc(wba_ev, 1)
            act.activation(wcol(IH, 8), w4[:, :, IH:24], ACT.Copy).then_inc(wba_ev, 1)
            act.wait_ge(cols_ev, 1)
            act.activation(cols_t[:, 0:53], ps[:, 5, 0:53], ACT.Copy)
            act.activation(cols_t[:, 53:54], ps[:, 5, 49:50], ACT.Copy, scale=SD ** -0.5)
            act.activation(cols_t[:, 54:55], ps[:, 5, 51:52], ACT.Copy, scale=GD ** -0.5).then_inc(cols_sb, 1)
            for a in range(8):
                if a + 1 < 8:
                    queries(a + 1)
                for e in range(a * PER_A, (a + 1) * PER_A):
                    w = entries[e][4]
                    act.wait_ge(dots_out, e + 1)
                    if e >= 3:
                        act.wait_ge(acc_out, e - 2)
                    act.activation(relu[:, e % 3, 0:w], ps[:, 4 + e % 4, 0:w], ACT.Relu).then_inc(relu_out, 1)

            def silu_of(u):
                act.wait_ge(conv_ev, u + 1)
                act.activation(QKV[:, u, :], cacc[:, u % 2, :], ACT.Silu).then_inc(silu_ev, 1)

            act.wait_ge(acc_out, len(entries))
            for u in range(12):
                n = N_QKV + u
                act.wait_ge(unit_done, ups[n] + 1)
                if u >= 2:
                    act.wait_ge(conv_ev, u - 1)
                act.activation(raw[:, u % 2, 3:3 + BANK], up_bank(n, 0), ACT.Copy)
                act.activation(raw[:, u % 2, 3 + BANK:3 + SEQ], up_bank(n, 1), ACT.Copy).then_inc(up_freed, 1)
                if u:
                    silu_of(u - 1)
            silu_of(11)
            act.wait_ge(silu_ev, 12)
            for v in range(16):
                n = N_Z + v
                act.wait_ge(unit_done, ups[n] + 1)
                if v >= 2:
                    act.wait_ge(spilled[v % 2], 16 * (v // 2))
                for half in range(HALVES):
                    ins = act.activation(cacc[:, v % 2, half * BANK:(half + 1) * BANK], up_bank(n, half),
                                         ACT.Silu if v < 4 else ACT.Copy)
                ins.then_inc(up_freed, 1)
                act.wait_ge(up_freed, ups[n] + 1)
                act.dma_start(z_dram[v] if v < 4 else d_dram[v - 4], cacc[:, v % 2, :]).then_inc(spilled[v % 2], 16)
            for s in spilled:
                act.wait_ge(s, 16 * 8)
            meet(1, act)

            g0a.mark(act.activation(th(beta), wcol(16, 4), ACT.Sigmoid), "beta")
            g0d.wait(act, "z")
            g0a.mark(act.activation(gtmp[:, 32:64], gtmp[:, 0:32], ACT.Abs), "abs")
            g0a.wait(act, "abs")
            g0a.mark(act.activation(gtmp[:, 32:64], gtmp[:, 32:64], ACT.Exp, scale=-1.0), "exp")
            g0a.wait(act, "exp")
            g0a.mark(act.activation(gtmp[:, 32:64], gtmp[:, 32:64], ACT.Ln, bias=1.0), "ln")
            g0a.mark(act.activation(alB[:, :], alB[:, :], ACT.Exp), "ea")
            for u in range(8):
                g0a.mark(act.activation(sqg[:, u, :], QKV[:, u, :], ACT.Square), f"sq{u}")
            g0p.wait(act, "stat")
            g0a.mark(act.activation(sd[:, 0:64], ps[:, 4, 0:64], ACT.Sqrt, bias=eps_t[:, 0:1]), "sd")
            g0p.wait(act, "sums")
            g0a.mark(act.activation(gtmp[:, 96:128], ps[:, 5, 0:32], ACT.Exp), "ed")
            g0a.mark(act.activation(erem[:, :], ps[:, 5, 32:64], ACT.Exp), "erem")
            g0a.mark(act.activation(lastb[:, :], ps[:, 5, 64:128], ACT.Exp), "last")
            meet(1, act)

            def prep(b, part):
                B = b % 2
                if part == "gq":
                    if b:
                        gp.wait(act, "w1", b - 1)
                    gp.wait(act, "diff", b)
                    ga.mark(act.activation(gam[:, 0, :], ps[:, 2, :], ACT.Exp), "gA", b)
                    ga.mark(act.activation(gam[:, 1, :], ps[:, 3, :], ACT.Exp), "gQ", b)
                elif part == "decay":
                    gd.wait(act, "Q1", b)
                    for j in range(2):
                        gp.wait(act, f"db{j}", b)
                        ga.mark(act.activation(gam[:, j, :], ps[:, 2 + j, :], ACT.Exp), f"e{j}", b)
                elif part[0] == "y":
                    gp.wait(act, part, b)
                    ga.mark(act.activation(Ym[:, :], ps[:, 0, :], ACT.Copy), part, b)
                elif part == "w":
                    if b >= 2:
                        sp_.wait(act, "o", 4 * (b - 1) - 1)
                    for j in range(2):
                        gp.wait(act, f"w{j}", b)
                        ga.mark(act.activation(wTt[:, B, j * BANK:(j + 1) * BANK], ps[:, 2 + j, :], ACT.Copy),
                                f"w{j}", b)

            def squares(t):
                sa_.wait(act, "ot", 2 * t + 1)
                if t:
                    ta.wait(act, f"q{t - 1}")
                for h in range(4):
                    ins = act.activation(gB[:, h * P:(h + 1) * P], QKV[:, h, t * P:(t + 1) * P], ACT.Square,
                                         accum_out=ss[:, 4 * t + h:4 * t + h + 1])
                ta.mark(ins, f"q{t}")

            def o_rms(i, t0, t1):
                ta.wait(act, f"q{t1 - 1}")
                ta.mark(act.activation(gtmp[:, 4 * t0:4 * t1], ss[:, 4 * t0:4 * t1], ACT.Sqrt, bias=eps_t[:, 0:1],
                                       scale=1.0 / GD), f"sd{i}")

            def dsa(part, e0, e1):
                if part == "on":
                    o_rms(0, 0, T_ON)
                elif part == "sq":
                    for e in range(e0, e1):
                        u, src, half = half_unit(e)
                        if e % 8 == 0:
                            act.wait_ge(qk_in[1 - e // 8], 16)
                        if e >= 2:
                            d0p.wait(act, f"st{e - 2}")
                        d0a.mark(act.activation(sqh[:, e % 2, :], src, ACT.Square), f"sq{e}")
                elif part == "sd":
                    d0p.wait(act, "st15")
                    d0a.mark(act.activation(sd[:, 0:128], ps[:, 7, 0:128], ACT.Sqrt, bias=eps_t[:, 0:1],
                                            scale=1.0 / SD), "sd")

            def scan_v(c):
                r = rows_of(c)[1]
                sp_.wait(act, "v", c)
                sa_.mark(act.activation(vn[r, :], ps[r, 4, :], ACT.Copy), "vn", c)
                if c and c % 2 == 0:
                    squares(c // 2 - 1)

            def scan_s(c):
                r, t = rows_of(c)[1], c // 2
                sp_.wait(act, "o", c)
                if c % 4 == 0:
                    gd.wait(act, "qd1", c // 4)
                sa_.mark(act.activation(QKV[r, 0:4, t * P:(t + 1) * P],
                                        ps[r, 5, :].rearrange("p (h c) -> p h c", c=P), ACT.Copy), "ot", c)

            gdn_order(prep, scan_v, scan_s, dsa)
            squares(TT - 1)
            o_rms(1, T_ON, TT)
            meet(1, act)
            for t in range(TT):
                act.wait_ge(v_tr, t + 1)
                act.activation(vtok[:, t, :], ps[:, 6 + t % 2, :], ACT.Copy).then_inc(v_ev, 1)
            tp.wait(act, f"tr{TT - 1}")
            act.activation(qO[SD:P, :, :], qD[SD:P, :, :], ACT.Copy).then_inc(q_odd, 1)
            meet(1, act)

            def exp_of(i):
                t, h = heads[i]
                n = (t + 1) * P
                act.wait_ge(mx, i + 1)
                if h == 0 and t >= 2:
                    act.wait_ge(drp, t - 1)
                act.activation(L[:, i % 3, 0:n], L[:, i % 3, 0:n], ACT.Exp, bias=sm8[:, i % 4:i % 4 + 1],
                               accum_out=sm8[:, 8 + 8 * (t % 2) + h:9 + 8 * (t % 2) + h]).then_inc(ex, 1)

            def pt_of(i):
                t, h = heads[i]
                if i >= 2:
                    act.wait_ge(pvs, i - 1)
                for k, (c, w) in enumerate(chunks((t + 1) * P)):
                    act.wait_ge(ptr, ptc[i] + k + 1)
                    act.activation(PT[:, i % 2, c:c + w], ps[:, 4 + (ptc[i] + k) % 2, 0:w], ACT.Copy).then_inc(pte, 1)

            N = len(heads)
            def y_tile(t):
                act.wait_ge(dtr, t + 1)
                act.activation(yB[:, :, t * P:(t + 1) * P], blocks(6 + t % 2), ACT.Copy).then_inc(dyb, 1)

            exp_of(0)
            for i in range(N):
                if i + 1 < N:
                    exp_of(i + 1)
                pt_of(i)
                if heads[i][1] == 5 and heads[i][0]:
                    y_tile(heads[i][0] - 1)
            y_tile(TT - 1)
            meet(1, act)

            for k in range(KT):
                src = yA[:, k, :] if k < 4 else yB[:, k - 4, :]
                act.activation(HS[:, 0, k, :], src, ACT.Copy).then_inc(hs_hi, 1)
            norm_act(act, norm_m)
            for a in range(8):
                n = N_KV + a
                act.wait_ge(unit_done, ups[n] + 1)
                dst = kX if a < 4 else vX
                act.activation(dst[:, a % 4, :], up_bank(n, 0)[:, 0:N_MEM], ACT.Copy).then_inc(up_freed, 1)
                if a == 3:
                    act.wait_ge(up_freed, ups[n] + 1)
                    xka.mark(act.activation(sqk[:, :, :], kX[:, :, :], ACT.Square), "sq")
            xkp.wait(act, "stat")
            xka.mark(act.activation(sd[:, 0:8], ps[:, 4, 0:8], ACT.Sqrt, bias=eps_t[:, 0:1], scale=1.0 / GD), "sd")
            for mt in range(2):
                xkp.wait(act, f"v{mt}")
                xka.mark(act.activation(vXt[:, mt, :], ps[:, 4 + mt, :], ACT.Copy), f"v{mt}")
            norm_act(act, norm2)
            for u in range(4):
                n = N_XQ + u
                act.wait_ge(unit_done, ups[n] + 1)
                act.activation(qX[:, u, 0:BANK], up_bank(n, 0), ACT.Copy)
                act.activation(qX[:, u, BANK:SEQ], up_bank(n, 1), ACT.Copy).then_inc(up_freed, 1)
            act.wait_ge(up_freed, ups[N_XO - 1] + 1)
            for u in range(4):
                x0a.mark(act.activation(sqx[:, u, :], qX[:, u, :], ACT.Square), f"sq{u}")
            x0p.wait(act, "stat")
            x0a.mark(act.activation(sd[:, 0:32], ps[:, 4, 0:32], ACT.Sqrt, bias=eps_t[:, 0:1], scale=1.0 / GD), "sd")

            def xprobs(t):
                act.wait_ge(xmx, t + 1)
                if t >= 2:
                    act.wait_ge(xptr, 2 * (t - 1))
                for h in range(4):
                    act.activation(Pb[:, t % 2, h * N_MEM:(h + 1) * N_MEM],
                                   ps[:, 2 * (t % 2) + h // 2, (h % 2) * N_MEM:(h % 2 + 1) * N_MEM], ACT.Exp,
                                   bias=sm8[:, 4 * (t % 2) + h:4 * (t % 2) + h + 1],
                                   accum_out=sm8[:, 8 + 4 * (t % 2) + h:9 + 4 * (t % 2) + h]).then_inc(xex, 1)

            xprobs(0)
            for t in range(TT):
                if t + 1 < TT:
                    xprobs(t + 1)
                if t == 4:
                    act.wait_ge(xo_, 4)
                for j in range(2):
                    act.wait_ge(xptr, 2 * t + j + 1)
                    act.activation(PTx[:, 2 * j:2 * j + 2, :, (t % 4) * P:(t % 4 + 1) * P],
                                   ps[:, 4 + j, :].rearrange("p (h m c) -> p h m c", h=2, c=P), ACT.Copy).then_inc(xpte, 1)
                if t % 4 == 3:
                    for h in range(4):
                        i = t - 3 + h
                        act.wait_ge(xo_, i + 1)
                        act.activation(HS[:, 0, h, (t // 4) * BANK:(t // 4 + 1) * BANK], ps[:, 6 + i % 2, :],
                                       ACT.Copy).then_inc(xohi, 1)
            norm_act(act, norm3)
            for s in (f_sil, f_hi):
                act.sem_inc(s, 1)
            with act.Fori(0, FFG) as g:
                for f in range(2):
                    act.wait_ge(unit_done, g * 4 + (UPS_FF + 2 * f + 1))
                    act.wait_ge(f_prod, g * 4 + (2 * f + 1))
                    for half in range(HALVES):
                        c = slice(half * BANK, (half + 1) * BANK)
                        act.activation(sil[:, c], ps[:, half, :], ACT.Silu).then_inc(f_sil, 1)
                    act.wait_ge(down_out, g * 16 + 16 * PAIRS_FF)
                    for half in range(HALVES):
                        c = slice(half * BANK, (half + 1) * BANK)
                        act.wait_ge(f_prod, g * 4 + (2 * f + half + 2))
                        act.activation(AS[:, f, 0, c], prod[:, c], ACT.Copy).then_inc(f_hi, 1)

        @block.vector
        def _(dve):
            def clink(ins):
                link("d", dve, d_chain, ins)

            norm_dve(dve, norm1, 1)
            for half in range(HALVES):
                dve.wait_ge(small_ev, half + 1)
                c = slice(half * BANK, (half + 1) * BANK)
                for r in (0, SD):
                    ins = dve.tensor_tensor(kI[r:r + SD, 1, c], ps[0:SD, half, :], kI[0:SD, 0, c].bitcast(F32),
                                            ALU.subtract)
            ins.then_inc(up_freed, 1)

            def queries_lo(a):
                for half in range(HALVES):
                    c = slice(half * BANK, (half + 1) * BANK)
                    dve.wait_ge(qi_hi, 2 * a + half + 1)
                    for j in range(2):
                        r, o = slice(SD * j, SD * j + SD), slice(SD * (1 - j), SD * (2 - j))
                        ins = dve.tensor_tensor(qI[o, a % 2, j, c], up_bank(a + 1, half)[r, :],
                                                qI[r, a % 2, j, c].bitcast(F32), ALU.subtract)
                ins.then_inc(qi_lo, 1)
                dve.wait_ge(qi_lo, a + 1)
                dve.sem_inc(up_freed, 1)

            queries_lo(0)
            dve.wait_ge(wba_ev, 2)
            for e, (a, j, t, c, w) in enumerate(entries):
                if e % PER_A == 0 and a + 1 < 8:
                    queries_lo(a + 1)
                acc = score[:, EOFF[t] + c:EOFF[t] + c + w]
                weight = wba[:, t * 24 + 2 * a + j:t * 24 + 2 * a + j + 1]
                dve.wait_ge(relu_out, e + 1)
                if e < PER_J:
                    dve.tensor_scalar(acc, relu[:, e % 3, 0:w], weight, None, ALU.mult).then_inc(acc_out, 1)
                else:
                    dve.wait_ge(acc_out, e + 1 - PER_J)
                    dve.scalar_tensor_tensor(acc, relu[:, e % 3, 0:w], weight, acc, ALU.mult,
                                             ALU.add).then_inc(acc_out, 1)
            dve.wait_ge(acc_out, len(entries))
            for t in range(TT):
                clink(dve.memset(score[0:CHUNK, EOFF[t + 1] - CHUNK:EOFF[t + 1]], TAKEN))
            clink(dve.memset(raw[:, 0, 0:3], 0.0))
            clink(dve.memset(raw[:, 1, 0:3], 0.0))

            taken = [0]

            def top_rounds(count):
                for i in range(taken[0], min(taken[0] + count, len(PAIRS) * ROUNDS)):
                    ts = PAIRS[i // ROUNDS]
                    for k, t in enumerate(ts):
                        if i:
                            dve.wait_ge(topk, 4 * i - 1 + k)
                        dve.max(top8[:, 8 * k:8 * k + 8], score[:, EOFF[t]:EOFF[t + 1]]).then_inc(topk, 1)
                    for k, t in enumerate(ts):
                        dve.wait_ge(topk, 4 * i + 1 + k)
                        s = score[:, EOFF[t]:EOFF[t + 1]]
                        dve.match_replace(s, top8[:, 8 * k:8 * k + 8], s, TAKEN).then_inc(topk, 1)
                    taken[0] = i + 1

            dve.wait_ge(cols_sb, 1)
            for u in range(12):
                dve.wait_ge(up_freed, ups[N_QKV + u] + 1)
                if u >= 2:
                    dve.wait_ge(silu_ev, u - 1)
                y, r = cacc[:, u % 2, :], raw[:, u % 2, :]
                clink(dve.tensor_scalar(y, r[:, 0:SEQ], tap(u, 0), None, ALU.mult))
                for k in range(1, 4):
                    ins = dve.scalar_tensor_tensor(y, r[:, k:k + SEQ], tap(u, k), y, ALU.mult, ALU.add)
                    if k < 3:
                        clink(ins)
                ins.then_inc(conv_ev, 1)
                top_rounds(2)
            for v in range(16):
                top_rounds(3)
            meet(2, dve)

            g0d.mark(dve.tensor_tensor(th(gtmp), wcol(20, 4), bc(dtB[:, :].unsqueeze(1), [P, TT, 4]), ALU.add), "z")
            g0d.wait(dve, "z")
            g0d.mark(dve.tensor_scalar(gtmp[:, 64:96], gtmp[:, 0:32], 0.0, None, ALU.max), "max")
            g0d.wait(dve, "max")
            g0a.wait(dve, "ln")
            g0d.mark(dve.tensor_tensor(gtmp[:, 64:96], gtmp[:, 64:96], gtmp[:, 32:64], ALU.add), "sp")
            g0d.wait(dve, "sp")
            g0a.wait(dve, "ea")
            g0d.mark(dve.scalar_tensor_tensor(th(gdec), th(gtmp, 64), -1.0, bc(alB[:, :].unsqueeze(1), [P, TT, 4]),
                                              ALU.mult, ALU.mult), "g")
            g0a.wait(dve, "sd")
            g0d.mark(dve.reciprocal(rs[:, 0:64], sd[:, 0:64]), "rs")
            g0d.wait(dve, "rs")
            g0d.mark(dve.tensor_scalar(rs[:, 0:32], rs[:, 0:32], GD ** -0.5, None, ALU.mult), "rq")
            g0a.wait(dve, "ed")
            g0d.mark(dve.scalar_tensor_tensor(nbed[:, :], gtmp[:, 96:128], -1.0, beta[:, :], ALU.mult, ALU.mult), "nbed")
            for e in range(16):
                u, c = e // 2, slice((e % 2) * BANK, (e % 2 + 1) * BANK)
                g0p.wait(dve, f"bc{e}")
                g0d.mark(dve.tensor_tensor(QKV[:, u, c], QKV[:, u, c], ps[:, e % 4, :], ALU.mult), f"n{e}")
            dve.wait_ge(consts, 2)
            clink(dve.scalar_tensor_tensor(negdist[:, :], negdist[:, :], -1.0, negdist[:, :], ALU.mult, ALU.min))
            clink(dve.memset(negdist[0:CHUNK, SEQ - CHUNK:SEQ], -BIG))
            meet(2, dve)

            def v4(t, c0=0):
                return t[:, c0:c0 + 4 * P].rearrange("p (h c) -> p h c", c=P)

            def v8(ap):
                return ap.rearrange("p (u c) -> p u c", c=CHUNK)

            def prep(b, part):
                B = b % 2
                if part == "in":
                    if b >= 2:
                        sp_.wait(dve, "o", 4 * (b - 1) - 1)
                    if b:
                        gp.wait(dve, "w1", b - 1)
                    for tl in range(2):
                        sc = slice(8 * b + 4 * tl, 8 * b + 4 * tl + 4)
                        gp.wait(dve, f"k{tl}", b)
                        for dst, by, name in ((nkbd[:, tl * BANK:(tl + 1) * BANK], nbed, "nk"),
                                              (kdec[:, B, tl * BANK:(tl + 1) * BANK], erem, "kd")):
                            gd.mark(dve.tensor_tensor(v4(dst), v4(ps[:, tl, :]), bc(by[:, sc].unsqueeze(2), [P, 4, P]),
                                                      ALU.mult), f"{name}{tl}", b)
                    for tl in range(2):
                        sc = slice(8 * b + 4 * tl, 8 * b + 4 * tl + 4)
                        gp.wait(dve, f"v{tl}", b)
                        gd.mark(dve.tensor_tensor(v4(vb[:, B, tl * BANK:(tl + 1) * BANK]), v4(ps[:, 2 + tl, :]),
                                                  bc(beta[:, sc].unsqueeze(2), [P, 4, P]), ALU.mult), f"vb{tl}", b)
                elif part == "mask":
                    gp.wait(dve, "GQ", b)
                    ga.wait(dve, "gA", b)
                    gl.wait(dve, "bM", b)
                    gd.mark(dve.tensor_tensor(Am[:, :], ps[:, 0, :], gam[:, 0, :], ALU.mult), "A1", b)
                    ga.wait(dve, "gQ", b)
                    gd.mark(dve.tensor_tensor(QKm[:, B, :], ps[:, 1, :], gam[:, 1, :], ALU.mult), "Q1", b)
                elif part == "decay":
                    for j in range(2):
                        ga.wait(dve, f"e{j}", b)
                        tok = slice((2 * b + j) * P, (2 * b + j + 1) * P)
                        gd.mark(dve.tensor_tensor(v4(qdec[:, B, j * BANK:(j + 1) * BANK]), QKV[:, 0:4, tok],
                                                  v4(gam[:, j, :]), ALU.mult), f"qd{j}", b)
                elif part == "x0":
                    gp.wait(dve, "x0", b)
                    gd.mark(dve.tensor_tensor(v8(TTm[:, B, :]), bc(I64[:, :].unsqueeze(1), [P, 8, CHUNK]),
                                              v8(ps[:, 0, :]), ALU.subtract), "TT0", b)
                elif part[0] == "z":
                    s = int(part[1])
                    gp.wait(dve, f"zt{s}", b)
                    gd.wait(dve, f"TT{s - 1}", b)
                    gd.mark(dve.tensor_tensor(TTm[:, B, :], TTm[:, B, :], ps[:, 1, :], ALU.subtract), f"TT{s}", b)
                    if s < 5:
                        gp.wait(dve, f"z{s}", b)
                        gl.wait(dve, "T0", b)
                        if s > 1:
                            gd.wait(dve, f"T{s - 1}", b)
                        gd.mark(dve.tensor_tensor(Tm[:, :], Tm[:, :], ps[:, 2, :], ALU.subtract), f"T{s}", b)
                    top_rounds(1)

            def scan_v(c):
                pass

            def scan_s(c):
                sp_.wait(dve, "s", c)
                new = S[:, (c + 1) % 2, :]
                if c:
                    sl_.wait(dve, "Sl", c - 1)
                    sd_.mark(dve.tensor_tensor(new, Sl[:, :], ps[:, 6, :], ALU.add), "S", c)
                else:
                    sd_.mark(dve.tensor_copy(new, ps[:, 6, :]), "S", c)

            def scale_o(i, t0, t1):
                ta.wait(dve, f"sd{i}")
                td.mark(dve.reciprocal(gtmp[:, 32 + 4 * t0:32 + 4 * t1], gtmp[:, 4 * t0:4 * t1]), f"r{i}")
                td.wait(dve, f"r{i}")
                ro = gtmp[:, 32 + 4 * t0:32 + 4 * t1].rearrange("p (t h) -> p t h", h=4)
                for h in range(4):
                    o = QKV[:, h, t0 * P:t1 * P].rearrange("p (t c) -> p t c", c=P)
                    td.mark(dve.tensor_tensor(o, o, bc(ro[:, :, h:h + 1], [P, t1 - t0, P]), ALU.mult), f"on{i}{h}")

            def logit_bias(t):
                s = score[:, EOFF[t]:EOFF[t + 1]]
                nd = negdist[:, (TT - 1 - t) * P:SEQ]
                if (t + 1) * P <= TOPK:
                    clink(dve.tensor_copy(s, nd))
                else:
                    clink(dve.tensor_scalar(s, s, TAKEN, -BIG, ALU.is_gt, ALU.mult))
                    clink(dve.tensor_tensor(s, s, nd, ALU.add))

            def dsa(part, e0, e1):
                if part == "top":
                    top_rounds(2)
                elif part == "on":
                    top_rounds(len(PAIRS) * ROUNDS)
                    scale_o(0, 0, T_ON)
                elif part == "sq":
                    for t in range(e0 // 2, e1 // 2):
                        logit_bias(t)
                elif part == "sd":
                    d0a.wait(dve, "sd")
                    d0d.mark(dve.reciprocal(rs[:, :], sd[:, :]), "rs")
                elif part == "bc":
                    for e in range(e0, e1):
                        u, src, half = half_unit(e)
                        d0p.wait(dve, f"bc{e}")
                        d0d.mark(dve.scalar_tensor_tensor(src, src, gK if u < 4 else gQ, ps[:, e % 4, :],
                                                          ALU.mult, ALU.mult), f"n{e}")

            gdn_order(prep, scan_v, scan_s, dsa)
            meet(2, dve)
            scale_o(1, T_ON, TT)
            dve.wait_ge(z_in, 16)
            dve.wait_ge(v_tr, TT)
            for t in range(TT):
                tp.wait(dve, f"tr{t}")
                td.mark(dve.scalar_tensor_tensor(yA[:, :, t * P:(t + 1) * P], blocks(t % 4), gO,
                                                 zS[:, :, t * P:(t + 1) * P], ALU.mult, ALU.mult), f"y{t}")
            meet(2, dve)

            def out_tile(t):
                dve.wait_ge(pvs, SH * (t + 1))
                sums = sm8[:, 8 + 8 * (t % 2):16 + 8 * (t % 2)]
                dve.reciprocal(sm8[:, 24:32], sums).then_inc(drp, 1)
                dve.wait_ge(drp, t + 1)
                if t:
                    dve.wait_ge(dtr, t)
                dve.tensor_tensor(dtok[:, :].rearrange("p (h c) -> p h c", c=SD),
                                  ps[:, 6 + t % 2, :].rearrange("p (h c) -> p h c", c=SD),
                                  bc(sm8[:, 24:32].unsqueeze(2), [P, SH, SD]), ALU.mult).then_inc(dnd, 1)

            for i, (t, h) in enumerate(heads):
                n = (t + 1) * P
                dve.wait_ge(lg, i + 1)
                if i >= 3:
                    dve.wait_ge(ptr, ptc[i - 2])
                dve.scalar_tensor_tensor(L[:, i % 3, 0:n], score[:, EOFF[t]:EOFF[t + 1]], 2.0 ** -(h + 1),
                                         psf[:, 2 * (i % 2) * BANK:2 * (i % 2) * BANK + n], ALU.mult,
                                         ALU.add).then_inc(Lw, 1)
                dve.wait_ge(Lw, i + 1)
                if i >= 4:
                    dve.wait_ge(ex, i - 3)
                dve.tensor_reduce(sm8[:, i % 4:i % 4 + 1], L[:, i % 3, 0:n], AX, ALU.max, negate=True).then_inc(mx, 1)
                if h == 2 and t:
                    out_tile(t - 1)
            out_tile(TT - 1)
            meet(2, dve)

            for k in range(KT):
                src = yA[:, k, :] if k < 4 else yB[:, k - 4, :]
                dve.wait_ge(hs_hi, k + 1)
                dve.tensor_tensor(HS[:, 1, k, :], src, HS[:, 0, k, :].bitcast(F32), ALU.subtract).then_inc(hs_lo, 1)
            dve.wait_ge(xr_in, 16)
            for p in range(4):
                down_dve(dve, 16 * p, first=(p == 0))
            norm_dve(dve, norm_m, 2)
            xka.wait(dve, "sd")
            xkd.mark(dve.reciprocal(rs[:, 0:8], sd[:, 0:8]), "rs")
            for j in range(2):
                xkp.wait(dve, f"bc{j}")
                kv = kX[:, 2 * j:2 * j + 2, :]
                xkd.mark(dve.scalar_tensor_tensor(kv, kv, gXK, ps[:, 6 + j, :].rearrange("p (a c) -> p a c", c=N_MEM),
                                                  ALU.mult, ALU.mult), f"n{j}")
            norm_dve(dve, norm2, 3)
            x0a.wait(dve, "sd")
            x0d.mark(dve.reciprocal(rs[:, 0:32], sd[:, 0:32]), "rs")
            for e in range(8):
                u, c = e // 2, slice((e % 2) * BANK, (e % 2 + 1) * BANK)
                x0p.wait(dve, f"bc{e}")
                x0d.mark(dve.scalar_tensor_tensor(qX[:, u, c], qX[:, u, c], gXQ, ps[:, e % 4, :],
                                                  ALU.mult, ALU.mult), f"n{e}")

            def xmax(t):
                dve.wait_ge(xlg, t + 1)
                if t >= 2:
                    dve.wait_ge(xex, 4 * (t - 1))
                dve.tensor_reduce(sm8[:, 4 * (t % 2):4 * (t % 2) + 4],
                                  psf[:, 2 * (t % 2) * BANK:2 * (t % 2 + 1) * BANK].rearrange("p (h c) -> p h c", c=N_MEM),
                                  AX, ALU.max, negate=True).then_inc(xmx, 1)

            xmax(0)
            for t in range(TT):
                if t + 1 < TT:
                    xmax(t + 1)
                dve.wait_ge(xex, 4 * (t + 1))
                if t:
                    dve.wait_ge(xpn, t)
                dve.reciprocal(sm8[:, 24:28], sm8[:, 8 + 4 * (t % 2):12 + 4 * (t % 2)]).then_inc(xr, 1)
                dve.wait_ge(xr, t + 1)
                pv = Pb[:, t % 2, :].rearrange("p (h c) -> p h c", c=N_MEM)
                dve.tensor_tensor(pv, pv, bc(sm8[:, 24:28].unsqueeze(2), [P, 4, N_MEM]), ALU.mult).then_inc(xpn, 1)
                if t % 4 == 3:
                    for h in range(4):
                        i = t - 3 + h
                        c = slice((t // 4) * BANK, (t // 4 + 1) * BANK)
                        dve.wait_ge(xohi, i + 1)
                        dve.tensor_tensor(HS[:, 1, h, c], ps[:, 6 + i % 2, :], HS[:, 0, h, c].bitcast(F32),
                                          ALU.subtract).then_inc(xolo, 1)
            for p in range(2):
                down_dve(dve, 16 * (4 + p))
            norm_dve(dve, norm3, 4)
            for s in (f_prod, f_lo):
                dve.sem_inc(s, 1)
            with dve.Fori(0, FFG) as g:
                for f in range(2):
                    dve.wait_ge(unit_done, g * 4 + (UPS_FF + 2 * f + 2))
                    dve.wait_ge(f_hi, g * 4 + (2 * f + 1))
                    dve.wait_ge(f_lo, g * 4 + (2 * f + 1))
                    for half in range(HALVES):
                        c = slice(half * BANK, (half + 1) * BANK)
                        dve.wait_ge(f_sil, g * 4 + (2 * f + half + 2))
                        dve.tensor_tensor(prod[:, c], sil[:, c], ps[:, 2 + half, :], ALU.mult).then_inc(f_prod, 1)
                    for half in range(HALVES):
                        c = slice(half * BANK, (half + 1) * BANK)
                        dve.wait_ge(f_hi, g * 4 + (2 * f + half + 2))
                        dve.tensor_tensor(AS[:, f, 1, c], prod[:, c], AS[:, f, 0, c].bitcast(F32),
                                          ALU.subtract).then_inc(f_lo, 1)
                down_dve(dve, g * 16 + 16 * PAIRS_FF)


_INS = ["x", "mem", "g_mix", "w_in", "conv_w", "a_log", "dt_bias", "g_gdn_out", "g_q_dsa", "g_k_dsa", "w_out",
        "g_xattn", "g_mem", "w_xq", "w_xkv", "g_xq", "g_xk", "w_xo", "g_ffn", "w_gu", "w_down"]


def kernel(**inputs):
    import numpy as np
    import concourse.bacc as bacc
    from concourse.bass_utils import run_bass_kernel_spmd

    nc = bacc.Bacc("TRN2", target_bir_lowering=False, num_devices=1)
    arrays, args = {}, []
    for name in _INS:
        a = np.ascontiguousarray(inputs[name])
        arrays[f"in_{name}"] = a
        args.append(nc.dram_tensor(f"in_{name}", a.shape, mybir.dt.from_np(a.dtype), kind="ExternalInput").ap())
    out = nc.dram_tensor("out_0", (1, SEQ, D), F32, kind="ExternalOutput").ap()
    build_layer(nc, *args, out)
    r = run_bass_kernel_spmd(nc, [arrays], core_ids=[0])
    return r.results[0]["out_0"]
```

```python
from contextlib import ExitStack

import concourse.bass as bass
from concourse import mybir

F32 = mybir.dt.float32
F32R = mybir.dt.float32r
ALU = mybir.AluOpType
ACT = mybir.ActivationFunctionType
AX = mybir.AxisListType.X

P = 128
SEQ, D, N_MEM = 1024, 1024, 256
CHUNK = 64
KT = D // P
TT = SEQ // P
BANK = 512
HALVES = SEQ // BANK
EPS = 1e-6
GH, GD = 4, 128
SH, SD = 8, 64
IH = 16
TOPK = 256
XH = 4
D_FF = 2816
KB = 1024
BIG = 1e30
TAKEN = -3e38
N_SMALL = 88

C_QKV, C_Z, C_B, C_DQ, C_DK, C_DV, C_IQ, C_IK = 0, 1536, 2048, 2056, 2568, 3080, 3592, 4616

EOFF = [P * t * (t + 1) // 2 for t in range(TT + 1)]
PAIRS = [(7, 2), (6, 3), (5, 4)]
ROUNDS = TOPK // 8
FFG = D_FF // 256
RING = 3


class Steps:

    def __init__(self, sem, names):
        self.sem, self.names, self.n = sem, list(names), 0
        self.at = {x: i + 1 for i, x in enumerate(self.names)}

    def value(self, name, rnd=0):
        return rnd * len(self.names) + self.at[name]

    def mark(self, ins, name, rnd=0):
        self.n += 1
        assert self.n == self.value(name, rnd), (name, rnd, self.n)
        ins.then_inc(self.sem, 1)
        return ins

    def wait(self, eng, name, rnd=0):
        eng.wait_ge(self.sem, self.value(name, rnd))


def chunks(n):
    return [(c, min(BANK, n - c)) for c in range(0, n, BANK)]


def build_layer(nc, x, mem, g_mix, w_in, conv_w, a_log, dt_bias, g_gdn_out, g_q_dsa, g_k_dsa, w_out,
                g_xattn, g_mem, w_xq, w_xkv, g_xq, g_xk, w_xo, g_ffn, w_gu, w_down, out):
    ctx = ExitStack()
    with ctx:
        base = (nc.sbuf_base + 63) // 64 * 64

        def at(name, shape, kb, dt=F32):
            return nc.alloc_sbuf_tensor_at(name, shape, dt, offset=base + int(kb * KB))

        def sem(name):
            return ctx.enter_context(nc.semaphore(name))

        def steps(name, names):
            return Steps(sem(name), names)

        ps = ctx.enter_context(nc.psum_tensor("ps", [P, 8, BANK], F32))
        z_dram = nc.dram_tensor("z_spill", (GH, P, SEQ), F32, kind="Internal").ap()
        kv_dram = nc.dram_tensor("kv_spill", (P, 2 * 4 * N_MEM), F32, kind="Internal").ap()
        d_dram = nc.dram_tensor("dsa_spill", (12, P, SEQ), F32, kind="Internal").ap()

        cur = [0.0]

        def small(name, cols):
            t = at(name, [P, cols], cur[0])
            cur[0] += (cols * 4 + 31) // 32 * 32 / KB
            return t

        ident = small("ident", P)
        Ublk = small("Ublk", P)
        Mblk = small("Mblk", P)
        Us = small("Us", CHUNK)
        Ms = small("Ms", CHUNK)
        I64 = small("I64", CHUNK)
        Lev = small("Lev", 6 * CHUNK)
        negdist = small("negdist", SEQ)
        gB = small("gB", D)
        half_ones = small("half_ones", 2 * P)
        blk2 = small("blk2", 2)
        ones1 = small("ones1", 2)
        zero1 = small("zero1", 2)
        eps_t = small("eps_t", 2)
        wba = small("wba", TT * 24)
        top8 = small("top8", 16)
        ss = small("ss", 128)
        sd = small("sd", 128)
        rs = small("rs", 128)
        beta = small("beta", 32)
        gdec = small("gdec", 32)
        nbed = small("nbed", 32)
        erem = small("erem", 32)
        lastb = small("lastb", 64)
        gtmp = small("gtmp", 32 * 4)
        dtB = small("dtB", 4)
        alB = small("alB", 4)
        sm8 = small("sm8", 64)
        stage = small("stage", P)
        cols_t = small("cols_t", 56)
        assert cur[0] <= 20, cur[0]

        WR = at("WR", [P, RING, 1024], 20)
        WS = at("WS", [P, RING, 2, 1024], 32, F32R)
        HS = at("HS", [P, 2, KT, SEQ], 56, F32R)

        X = at("X", [P, TT, D], 120)
        xn = at("xn", [P, 2, D], 152)
        junk = at("junk", [P, 2, D], 160)
        score = at("score", [P, EOFF[TT]], 168)
        qI = at("qI", [P, 2, 2, SEQ], 124, F32R)
        kI = at("kI", [P, 2, SEQ], 186, F32R)
        relu = at("relu", [P, 3, BANK], 198)
        wT = at("wT", [24, SEQ], 120)
        QKV = at("QKV", [P, 12, SEQ], 120)
        raw = at("raw", [P, 2, SEQ + 4], 186)
        cacc = at("cacc", [P, 2, SEQ], 195)
        sqg = at("sqg", [P, SEQ], 203.5)
        kdec = at("kdec", [P, 2, 8 * P], 56)
        vb = at("vb", [P, 2, 8 * P], 64)
        wTt = at("wTt", [P, 2, 8 * P], 72)
        qdec = at("qdec", [P, 2, 8 * P], 80)
        TTm = at("TTm", [P, 2, BANK], 88)
        QKm = at("QKm", [P, 2, BANK], 92)
        nkbd = at("nkbd", [P, 8 * P], 96)
        Tm = at("Tm", [P, BANK], 100)
        Xm = at("Xm", [P, BANK], 102)
        Ym = at("Ym", [P, BANK], 104)
        Am = at("Am", [P, BANK], 106)
        gam = at("gam", [P, 2, BANK], 108)
        gMU = at("gMU", [P, 2, BANK], 112)
        S = at("S", [P, 2, BANK], 116)
        yA = at("yA", [P, 4, SEQ], 186)
        Sl = at("Sl", [P, BANK], 202)
        vn = at("vn", [P, BANK], 204)
        zS = at("zS", [P, 4, SEQ], 152)
        qD = at("qD", [P, 4, SEQ], 100)
        qO = at("qO", [P, 4, SEQ], 116)
        kD = at("kD", [P, 4, SEQ], 136)
        sqh = at("sqh", [P, 2, BANK], 96)
        vraw = at("vraw", [P, 4, SEQ], 186)
        yB = at("yB", [P, 4, SEQ], 152)
        vtok = at("vtok", [P, TT, BANK], 56)
        L = at("L", [P, 3, SEQ], 72)
        PT = at("PT", [P, 2, SEQ], 84)
        dtok = at("dtok", [P, BANK], 92)
        KW = at("KW", [P, 2, 1024], 168)
        M0 = at("M0", [P, 2, D], 176)
        MT = at("MT", [P, KT, N_MEM], 184)
        kr = at("kr", [P, 4, N_MEM], 194)
        vr = at("vr", [P, 4, N_MEM], 198)
        gM = at("gM", [P, D], 202)
        sqk = at("sqk", [P, 4, N_MEM], 176)
        kv0 = at("kv0", [P, 2, 4 * N_MEM], 140)
        kvX = at("kvX", [P, 2, 4 * N_MEM], 192)
        qX = at("qX", [P, 4, SEQ], 168)
        sqx = at("sqx", [P, 4, SEQ], 152)
        Pb = at("Pb", [P, 2, 4 * N_MEM], 72)
        PTx = at("PTx", [P, 4, 2, BANK], 104)
        AS = at("AS", [P, 2, 2, SEQ], 168, F32R)
        sil = at("sil", [P, SEQ], 184)
        prod = at("prod", [P, SEQ], 188)

        psf = ps[:, :, :].rearrange("p b c -> p (b c)")

        w_in0, w_out0, w_xq0, w_xkv0, w_xo0, w_gu0, w_dn0 = (
            a[0] for a in (w_in, w_out, w_xq, w_xkv, w_xo, w_gu, w_down))

        def cols_of(w, c, n=P):
            return w[:, bass.ds(c, n)].rearrange("(k p) c -> p k c", p=P)

        units = ["small"]
        units += [cols_of(w_in0, C_IQ + a * P) for a in range(8)]
        N_QKV = len(units)
        units += [cols_of(w_in0, C_QKV + a * P) for a in range(12)]
        N_Z = len(units)
        units += [cols_of(w_in0, C_Z + a * P) for a in range(4)]
        units += [cols_of(w_in0, C_DQ + a * P) for a in range(12)]
        N_OUT = len(units)
        units += [w_out0[k * P:(k + 1) * P, :] for k in range(8)]
        N_KV = len(units)
        units += [cols_of(w_xq0, a * P) for a in range(4)]
        N_XO = len(units)
        units += [w_xo0[k * P:(k + 1) * P, :] for k in range(4)]
        N_FF = len(units)
        PER = 6
        assert PER % RING == 0

        ups, pairs, freed = {}, {}, []
        for n in range(N_FF):
            if N_OUT <= n < N_KV or n >= N_XO:
                pairs.setdefault(n - (n - N_OUT) % 2 if n < N_KV else n - (n - N_XO) % 2, len(pairs))
                freed.append(("pair", len(pairs)))
            else:
                ups[n] = len(ups)
                freed.append(("up", len(ups)))
        UPS_FF, PAIRS_FF = len(ups), len(pairs)
        landed = [sem(f"w_landed{i}") for i in range(RING)]
        landed_at, have = [], [0] * RING
        for n in range(N_FF):
            have[n % RING] += 32 if n == 0 else 16
            landed_at.append(have[n % RING])
        w_hi = sem("w_hi")
        w_split = sem("w_split")
        unit_done = sem("unit_done")
        down_out = sem("down_out")
        down_add = sem("down_add")
        up_freed = sem("up_freed")
        consts = sem("consts")
        x_in = [sem(f"x_in{i}") for i in range(4)]
        row_in = sem("row_in")
        gB_in = sem("gB_in")
        met = sem("met")
        meetings = [0, 0, 0]

        def meet(i, eng):
            meetings[i] += 1
            eng.drain().then_inc(met, 1)
            eng.wait_ge(met, 3 * meetings[i])

        a_chain, d_chain, p_chain = sem("act_chain"), sem("dve_chain"), sem("pool_chain")
        linked = {"a": 0, "d": 0, "p": 0}

        def link(key, eng, chain, ins):
            linked[key] += 1
            ins.then_inc(chain, 1)
            eng.wait_ge(chain, linked[key])

        class Norm:
            def __init__(self, tag, X, n, dst, ready, nb=4):
                self.X, self.n, self.dst, self.ready, self.nb = X, n, dst, ready, nb
                self.ss, self.sd, self.rs, self.xn, self.tr, self.hi, self.lo = (
                    sem(f"{tag}_{x}") for x in ("ss", "sd", "rs", "xn", "tr", "hi", "lo"))

            def bank(self, t, j):
                return 2 * (t % self.nb) + j

        def dst_of(m, part, t, j):
            return m.dst[:, part, 4 * j:4 * j + 4, t * P:(t + 1) * P]

        def blocks(bank):
            return ps[:, bank, :].rearrange("p (k c) -> p k c", c=P)

        def norm_act(act, m, after=None):
            def evac(t):
                for j in range(2):
                    act.wait_ge(m.tr, 2 * t + j + 1)
                    act.activation(dst_of(m, 0, t, j), blocks(m.bank(t, j)), ACT.Copy).then_inc(m.hi, 1)
            for t in range(m.n):
                m.ready(act, t)
                if t >= 2:
                    act.wait_ge(m.ss, t - 1)
                act.activation(junk[:, t % 2, :], m.X[:, t, :], ACT.Square,
                               accum_out=ss[:, t:t + 1]).then_inc(m.ss, 1)
                act.wait_ge(m.ss, t + 1)
                act.activation(sd[:, t:t + 1], ss[:, t:t + 1], ACT.Sqrt, bias=eps_t[:, 0:1],
                               scale=1.0 / D).then_inc(m.sd, 1)
                if t:
                    evac(t - 1)
                if after:
                    after(t)
            evac(m.n - 1)

        def norm_dve_lo(dve, m, t):
            for j in range(2):
                dve.wait_ge(m.hi, 2 * t + j + 1)
                dve.tensor_tensor(dst_of(m, 1, t, j), blocks(m.bank(t, j)),
                                  dst_of(m, 0, t, j).bitcast(F32), ALU.subtract).then_inc(m.lo, 1)

        def norm_dve_tile(dve, m, t, g_count):
            if t == 0:
                dve.wait_ge(gB_in, 16 * g_count)
            dve.wait_ge(m.sd, t + 1)
            dve.reciprocal(rs[:, t:t + 1], sd[:, t:t + 1]).then_inc(m.rs, 1)
            dve.wait_ge(m.rs, t + 1)
            if t >= 2:
                dve.wait_ge(m.tr, 2 * (t - 1))
            dve.scalar_tensor_tensor(xn[:, t % 2, :], m.X[:, t, :], rs[:, t:t + 1], gB[:, :],
                                     ALU.mult, ALU.mult).then_inc(m.xn, 1)
            if t:
                norm_dve_lo(dve, m, t - 1)

        def norm_dve(dve, m, g_count):
            for t in range(m.n):
                norm_dve_tile(dve, m, t, g_count)
            norm_dve_lo(dve, m, m.n - 1)

        def norm_pe_tile(pe, m, t):
            pe.wait_ge(m.xn, t + 1)
            if t >= m.nb:
                pe.wait_ge(m.lo, 2 * (t + 1 - m.nb))
            for j in range(2):
                for k in range(4):
                    mm = pe.transpose(ps[:, m.bank(t, j), k * P:(k + 1) * P],
                                      xn[:, t % 2, (4 * j + k) * P:(4 * j + k + 1) * P], ident[:, :])
                mm.then_inc(m.tr, 1)

        def norm_pe(pe, m):
            for t in range(m.n):
                norm_pe_tile(pe, m, t)

        def up_pe(pe, n, src, width, ncol=P, between=None):
            m = ups[n]
            pe.wait_ge(w_split, n + 1)
            if m >= 2:
                pe.wait_ge(up_freed, m - 1)
            for half, (c, w) in enumerate(chunks(width)):
                acc = ps[0:ncol, 2 * (m % 2) + half, 0:w]
                for k in range(KT):
                    hi, lo = (WS[:, n % RING, s, k * ncol:(k + 1) * ncol] for s in (0, 1))
                    pe.matmul(acc, lo, src[:, 0, k, c:c + w], start=(k == 0), stop=False)
                    pe.matmul(acc, hi, src[:, 1, k, c:c + w], start=False, stop=False)
                    mm = pe.matmul(acc, hi, src[:, 0, k, c:c + w], start=False, stop=(k == KT - 1))
                    if between and half * KT + k + 1 < HALVES * KT:
                        between(half * KT + k)
            mm.then_inc(unit_done, 1)

        def up_bank(n, half):
            return ps[:, 2 * (ups[n] % 2) + half, :]

        def down_pe(pe, slots, split, blk, lhs, ready, after=None):
            for r in range(4):
                for s in range(2):
                    if r == 0:
                        pe.wait_ge(w_split, split - 1 + s)
                        ready(s)
                    for q in range(4):
                        t, h = (4 * r + q) // 2, q % 2
                        if s == 0 and (r or blk is not None):
                            pe.wait_ge(down_add, (0 if blk is None else blk) + 4 * r + q - 3)
                        whi, wlo = (WS[:, slots[s], a, h * BANK:(h + 1) * BANK] for a in (0, 1))
                        xhi, xlo = lhs(s, t)
                        acc = ps[:, 4 + q, :]
                        pe.matmul(acc, xlo, whi, start=(s == 0), stop=False)
                        pe.matmul(acc, xhi, wlo, start=False, stop=False)
                        mm = pe.matmul(acc, xhi, whi, start=False, stop=(s == 1))
                        if s == 1:
                            mm.then_inc(down_out, 1)
                if after:
                    after(r)

        def down_dve(dve, blk, first=False, after=None):
            for o in range(16):
                t, h = o // 2, o % 2
                dve.wait_ge(down_out, blk + o + 1)
                if not first:
                    dve.wait_ge(down_add, blk + o - 15)
                xs = X[:, t, h * BANK:(h + 1) * BANK]
                dve.tensor_tensor(xs, xs, ps[:, 4 + o % 4, :], ALU.add).then_inc(down_add, 1)
                if after and h:
                    after(t)

        small_ev = sem("small_evac")
        wba_tr, wba_ev = sem("wba_tr"), sem("wba_ev")
        qi_hi = sem("qi_hi")
        qi_lo = sem("qi_lo")
        dots_out, relu_out, acc_out = sem("dots_out"), sem("relu_out"), sem("score_acc")
        entries = [(a, j, t, c, w) for a in range(8) for j in range(2) for t in range(TT)
                   for c, w in chunks((t + 1) * P)]
        PER_A = len(entries) // 8
        PER_J = PER_A // 2
        conv_ev, silu_ev = sem("conv"), sem("silu")
        spilled = [sem("spilled0"), sem("spilled1")]
        topk = sem("topk")
        cols_ev = sem("cols_tr")
        cols_sb = sem("cols_sb")

        norm1 = Norm("n1", X, TT, HS, lambda e, t: e.wait_ge(x_in[t // 2], 16), 2)
        nm_ss, nm_sd, nm_rs, nm_xn, nm_tr, nm_ev = (sem("nm_" + x) for x in ("ss", "sd", "rs", "xn", "tr", "ev"))
        kw_in = [sem("kw_in0"), sem("kw_in1")]
        kv_done, kv_ev = sem("kv_done"), sem("kv_evac")
        gM_in, kv_out, kv_in = sem("gM_in"), sem("kv_stored"), sem("kv_in")
        m_in = sem("mem_in")
        norm2 = Norm("n2", X, TT, HS, lambda e, t: e.wait_ge(down_add, 16 * 3 + 2 * t + 2), 2)
        norm3 = Norm("n3", X, TT, HS, lambda e, t: e.wait_ge(down_add, 16 * 5 + 2 * t + 2), 2)

        LV = range(1, 6)
        g0p = steps("g0_pe", ["sums"] + [f"st{u}" for u in range(8)] + [f"bc{e}" for e in range(16)])
        g0a = steps("g0_act", ["beta", "abs", "exp", "ln", "ea"] + [f"sq{u}" for u in range(8)]
                    + ["sd", "ed", "erem", "last"])
        g0d = steps("g0_dve", ["z", "max", "sp", "g", "rs", "rq", "nbed"] + [f"n{e}" for e in range(16)])
        gp = steps("gdn_pe", ["k0", "k1", "v0", "v1", "GQ", "diff", "db0", "db1", "x0"]
                   + [f"{x}{s}" for s in LV for x in (("y", "zt", "z") if s < 5 else ("y", "zt"))] + ["w0", "w1"])
        gd = steps("gdn_dve", ["nk0", "kd0", "nk1", "kd1", "vb0", "vb1", "A1", "Q1", "qd0", "qd1", "TT0"]
                   + [f"{x}{s}" for s in LV for x in (("TT", "T") if s < 5 else ("TT",))])
        ga = steps("gdn_act", ["gA", "gQ", "e0", "e1"] + [f"y{s}" for s in LV] + ["w0", "w1"])
        gl = steps("gdn_pool", ["gM", "gU", "bM", "A", "Q", "X0", "T0"] + [f"X{s}" for s in LV])
        sp_, sd_ = steps("scan_pe", ["v", "s", "o"]), steps("scan_dve", ["S"])
        sa_, sl_ = steps("scan_act", ["vn", "ot"]), steps("scan_pool", ["Sl"])
        tp = steps("gpost_pe", [f"tr{i}" for i in range(TT)])
        T_ON = 6
        td = steps("gpost_dve", ["r0"] + [f"on0{h}" for h in range(4)] + ["r1"] + [f"on1{h}" for h in range(4)]
                   + [f"y{i}" for i in range(TT)])
        ta = steps("gpost_act", [f"q{t}" for t in range(T_ON)] + ["sd0"] + [f"q{t}" for t in range(T_ON, TT)] + ["sd1"])
        z_in = sem("z_in")

        qk_in = [sem(f"qk_in{i}") for i in range(3)]
        d0p = steps("d0_pe", [f"st{e}" for e in range(16)] + [f"bc{e}" for e in range(16)])
        d0a = steps("d0_act", [f"sq{e}" for e in range(16)] + ["sd"])
        d0d = steps("d0_dve", ["rs"] + [f"n{e}" for e in range(16)])
        q_odd, q_pad = sem("q_odd"), sem("q_pad")
        v_tr, v_ev = sem("v_tr"), sem("v_ev")
        lg, Lw, mx, ex, ptr, pte, pvs = (sem("dsa_" + x) for x in ("lg", "L", "max", "exp", "ptr", "pt", "pv"))
        heads = [(t, h) for t in range(TT) for h in range(SH)]
        ptc = [0]
        for t, h in heads:
            ptc.append(ptc[-1] + len(chunks((t + 1) * P)))
        drp, dnd, dtr, dyb = sem("dsa_r"), sem("dsa_norm"), sem("dsa_tr"), sem("dsa_y")
        hs_hi, hs_lo = sem("hs_hi"), sem("hs_lo")
        xr_in = sem("x_again")

        xkp = steps("xk_pe", ["stat", "v0", "v1", "bc0", "bc1"])
        xka = steps("xk_act", ["sq", "sd", "v0", "v1"])
        xkd = steps("xk_dve", ["rs", "n0", "n1"])
        x0p = steps("xq_pe", [f"st{u}" for u in range(4)])
        x0a = steps("xq_act", [f"sq{u}" for u in range(4)] + ["sd"])
        x0d = steps("xq_dve", ["rs"])
        x_max = sem("xa_rawmax")
        xlg, xmx, xex, xr, xpn, xptr, xpte = (sem("xa_" + x) for x in ("lg", "max", "exp", "r", "pn", "ptr", "pt"))
        xo_, xohi, xolo = sem("xa_o"), sem("xa_ohi"), sem("xa_olo")

        f_sil, f_prod, f_hi, f_lo = sem("ff_silu"), sem("ff_prod"), sem("ff_hi"), sem("ff_lo")
        out_sem = sem("out_stored")

        def bc(ap, shape):
            return ap.to_broadcast(shape)

        PREP = ["in", "gq", "mask", "decay", "x0"] + [f"{x}{s}" for s in LV for x in "yz"] + ["w"]

        def half_unit(e):
            u, half = e // 2, e % 2
            return u, (kD if u < 4 else qD)[:, u % 4, half * BANK:(half + 1) * BANK], half

        DSA_PARTS = {0: ("top", 0, 0), 1: ("top", 0, 0), 2: ("on", 0, 0), 3: ("sq", 0, 8), 4: ("sq", 8, 16),
                     5: ("sd", 0, 0), 6: ("bc", 0, 8), 7: ("bc", 8, 16)}

        def gdn_order(prep, scan_v, scan_s, dsa):
            for part in PREP:
                prep(0, part)
            for c in range(SEQ // CHUNK):
                parts = PREP[4 * (c % 4):4 * (c % 4) + 4] if c // 4 < 3 else []
                scan_v(c)
                for part in parts[:2]:
                    prep(c // 4 + 1, part)
                if 2 * (c - 12) in DSA_PARTS:
                    dsa(*DSA_PARTS[2 * (c - 12)])
                scan_s(c)
                for part in parts[2:]:
                    prep(c // 4 + 1, part)
                if 2 * (c - 12) + 1 in DSA_PARTS:
                    dsa(*DSA_PARTS[2 * (c - 12) + 1])

        MEET_MIX, MEET_DSA = 1, 4
        block = ctx.enter_context(nc.Block())

        @block.sync
        def _(sp):
            def load(n, view=None, split_at=None):
                if n >= RING:
                    sp.wait_ge(w_split, n + 1 - RING)
                slot = n % RING
                if n == 0:
                    for c, w, d in ((C_IK, 80, 0), (C_B, 8, 80)):
                        sp.dma_start(WR[:, 0, 0:KT * N_SMALL].rearrange("p (k c) -> p k c", c=N_SMALL)[:, :, d:d + w],
                                     cols_of(w_in0, c, w)).then_inc(landed[0], 16)
                elif N_OUT <= n < N_KV or n >= N_XO:
                    sp.dma_start(WR[:, slot, :], units[n]).then_inc(landed[slot], 16)
                else:
                    sp.dma_start(WR[:, slot, :].rearrange("p (k c) -> p k c", c=P), units[n]).then_inc(landed[slot], 16)

            xv = x[0].rearrange("(t p) d -> p t d", p=P)

            def load_kv(a):
                if a >= 2:
                    sp.wait_ge(kv_done, a - 1)
                sp.dma_start(KW[:, a % 2, :].rearrange("p (k c) -> p k c", c=P),
                             cols_of(w_xkv0, a * P)).then_inc(kw_in[a % 2], 16)

            sp.dma_start(M0[:, :, :], mem[0].rearrange("(t p) d -> p t d", p=P)).then_inc(m_in, 16)
            sp.dma_start(gM[:, :], g_mem[0:1, :].to_broadcast([P, D])).then_inc(gM_in, 16)
            for i in range(4):
                sp.dma_start(X[:, 2 * i:2 * i + 2, :], xv[:, 2 * i:2 * i + 2, :]).then_inc(x_in[i], 16)
                if i == 0:
                    sp.dma_start(gB[:, :], g_mix[0:1, :].to_broadcast([P, D])).then_inc(gB_in, 16)
                    load_kv(0)
                    load_kv(1)
            sp.dma_start(stage[0:48, :], conv_w[0].rearrange("k (u p) -> (k u) p", p=P)).then_inc(row_in, 16)
            for r, g, n in ((48, g_gdn_out, P), (49, g_q_dsa, SD), (50, g_k_dsa, SD), (51, g_xq, P), (52, g_xk, P)):
                for c in range(0, P, n):
                    sp.dma_start(stage[r:r + 1, c:c + n], g[0:1, :]).then_inc(row_in, 16)
            sp.dma_start(dtB[:, :], dt_bias[0:1, :].to_broadcast([P, 4])).then_inc(row_in, 16)
            sp.dma_start(alB[:, :], a_log[0:1, :].to_broadcast([P, 4])).then_inc(row_in, 16)
            for n in range(RING):
                load(n)
            for a in range(2, 8):
                load_kv(a)
            for n in range(RING, RING + 2):
                load(n)
            xkd.wait(sp, "n1")
            xka.wait(sp, "v1")
            sp.dma_start(kv_dram[:, :], kv0[:, :, :].rearrange("p a c -> p (a c)")).then_inc(kv_out, 16)
            for n in range(RING + 2, N_OUT + 2 * RING):
                load(n)
            sp.wait_ge(kv_out, 16)
            for s in spilled:
                sp.wait_ge(s, 16 * 8)
            sp.wait_ge(met, 3 * MEET_MIX)
            back = d_dram.rearrange("(i u) p c -> i p u c", u=4)
            sp.dma_start(vraw[:, :, :], back[2]).then_inc(qk_in[2], 16)
            gp.wait(sp, "w1", 3)
            sp.dma_start(kD[:, :, :], back[1]).then_inc(qk_in[1], 16)
            sp.dma_start(qD[:, :, :], back[0]).then_inc(qk_in[0], 16)
            sp.dma_start(zS[:, :, :], z_dram.rearrange("u p c -> p u c")).then_inc(z_in, 16)
            ta.wait(sp, f"q{TT - 1}")
            sp.dma_start(gB[:, :], g_xattn[0:1, :].to_broadcast([P, D])).then_inc(gB_in, 16)
            sp.wait_ge(met, 3 * MEET_DSA)
            sp.dma_start(X[:, :, :], xv).then_inc(xr_in, 16)
            sp.wait_ge(hs_lo, 4)
            sp.dma_start(kvX[:, :, :].rearrange("p a c -> p (a c)"), kv_dram[:, :]).then_inc(kv_in, 16)
            for n in range(N_OUT + 2 * RING, N_KV + 2 * RING):
                load(n)
            sp.wait_ge(norm2.xn, TT)
            sp.dma_start(gB[:, :], g_ffn[0:1, :].to_broadcast([P, D])).then_inc(gB_in, 16)
            for n in range(N_KV + 2 * RING, N_FF):
                load(n)
            with sp.Fori(0, FFG) as g:
                for j in range(PER):
                    slot = (N_FF + j) % RING
                    sp.wait_ge(w_split, g * PER + (N_FF + j + 1 - RING))
                    if j < 4:
                        c = g * 256 + (j // 2) * P + (j % 2) * D_FF
                        sp.dma_start(WR[:, slot, :].rearrange("p (k c) -> p k c", c=P),
                                     cols_of(w_gu0, c)).then_inc(landed[slot], 16)
                    else:
                        sp.dma_start(WR[:, slot, :], w_dn0[bass.ds(g * 256 + (j - 4) * P, P), :]).then_inc(landed[slot], 16)
            for t in range(TT):
                sp.wait_ge(down_add, 16 * (PAIRS_FF + FFG - 1) + 2 * t + 2)
                sp.dma_start(out[0, t * P:(t + 1) * P, :], X[:, t, :]).then_inc(out_sem, 16)
            sp.wait_ge(out_sem, 16 * TT)

        @block.gpsimd
        def _(pool):
            def step(ins):
                link("p", pool, p_chain, ins)

            def select(tile, pattern, base_, cm, op=ALU.is_ge, fill=0.0):
                step(pool.affine_select(out=tile, in_=tile, pattern=pattern, compare_op=op, fill=fill,
                                        base=base_, channel_multiplier=cm))

            pool.memset(eps_t[:, :], EPS)
            step(pool.memset(ident[:, :], 0.0))
            select(ident[:, :], [[-1, P]], 0, 1, ALU.not_equal, 1.0)
            pool.memset(ones1[:, :], 1.0)
            pool.memset(zero1[:, :], 0.0)
            pool.memset(blk2[:, :], 0.0)
            pool.memset(half_ones[:, :], 0.0)
            pool.memset(Lev[:, :], 0.0)
            pool.memset(Mblk[:, :], 1.0)
            step(pool.memset(Ublk[:, :], 1.0))
            pool.drain().then_inc(consts, 1)

            def split(n_split, slot, land, free, cols):
                pool.wait_ge(landed[slot], land)
                if free is not None:
                    pool.wait_ge(free[0], free[1])
                hi, lo, w = WS[:, slot, 0, 0:cols], WS[:, slot, 1, 0:cols], WR[:, slot, 0:cols]
                pool.tensor_tensor(hi, w, bc(zero1[:, 0:1], [P, cols]), ALU.add).then_inc(w_hi, 1)
                pool.wait_ge(w_hi, n_split + 1)
                pool.tensor_tensor(lo, w, hi.bitcast(F32), ALU.subtract).then_inc(w_split, 1)

            def split_of(n):
                free = None
                if n >= RING:
                    kind, count = freed[n - RING]
                    free = (unit_done, count) if kind == "up" else (down_out, 16 * count)
                split(n, n % RING, landed_at[n], free, KT * N_SMALL if n == 0 else 1024)

            for n in range(RING):
                split_of(n)
            select(Ublk[:, :], [[1, P]], 0, -1)
            step(pool.memset(Ublk[0:CHUNK, CHUNK:P], 0.0))
            select(Mblk[:, :], [[-1, P]], -1, 1)
            step(pool.memset(Mblk[CHUNK:P, 0:CHUNK], 0.0))
            pool.memset(half_ones[0:CHUNK, 0:P], 1.0)
            pool.memset(half_ones[CHUNK:P, P:2 * P], 1.0)
            pool.memset(blk2[0:CHUNK, 0:1], 1.0)
            pool.memset(blk2[CHUNK:P, 1:2], 1.0)
            for r in (0, CHUNK):
                rows = slice(r, r + CHUNK)
                for dst, src in ((Us, Ublk), (Ms, Mblk), (I64, ident)):
                    pool.tensor_copy(dst[rows, :], src[rows, r:r + CHUNK])
                for s in range(6):
                    w = 1 << s
                    lev = Lev[rows, s * CHUNK:(s + 1) * CHUNK].rearrange("p (b c) -> p b c", c=2 * w)[:, :, 0:w]
                    nb = CHUNK // (2 * w)
                    step(pool.memset(lev, 1.0))
                    select(lev, [[-2 * w, nb], [0, w]], -w, 1)
                    select(lev, [[2 * w, nb], [0, w]], 2 * w - 1, -1)
            step(pool.iota(negdist[:, :], pattern=[[-1, SEQ]], base=SEQ - P, channel_multiplier=1,
                           allow_small_or_imprecise_dtypes=True))
            pool.drain().then_inc(consts, 1)
            for n in range(RING, N_OUT + RING):
                split_of(n)

            def v8(ap):
                return ap.rearrange("p (u c) -> p u c", c=CHUNK)

            def mask_of(m):
                return bc(m.unsqueeze(1), [P, 8, CHUNK])

            def prep(b, part):
                B = b % 2
                if part == "in":
                    if b:
                        gp.wait(pool, "w1", b - 1)
                    else:
                        g0d.wait(pool, "g")
                        g0a.wait(pool, "beta")
                    for dst, by, m, name in ((gMU[:, 0, :], gdec, Ms, "gM"), (gMU[:, 1, :], gdec, Us, "gU"),
                                             (Xm[:, :], beta, Ms, "bM")):
                        if b == 0 and name == "gM":
                            pool.wait_ge(met, 3 * MEET_MIX)
                        gl.mark(pool.tensor_tensor(v8(dst), bc(by[:, 8 * b:8 * b + 8].unsqueeze(2), [P, 8, CHUNK]),
                                                   mask_of(m[:, :]), ALU.mult), name, b)
                elif part == "mask":
                    gd.wait(pool, "A1", b)
                    gl.wait(pool, "bM", b)
                    gl.mark(pool.tensor_tensor(Am[:, :], Am[:, :], Xm[:, :], ALU.mult), "A", b)
                    gd.wait(pool, "Q1", b)
                    gl.mark(pool.tensor_tensor(v8(QKm[:, B, :]), v8(QKm[:, B, :]), mask_of(Us[:, :]), ALU.mult), "Q", b)
                    gl.wait(pool, "A", b)
                    gl.mark(pool.tensor_tensor(v8(Xm[:, :]), v8(Am[:, :]), mask_of(Lev[:, 0:CHUNK]), ALU.mult), "X0", b)
                    gl.wait(pool, "X0", b)
                    gl.mark(pool.tensor_tensor(v8(Tm[:, :]), mask_of(I64[:, :]), v8(Xm[:, :]), ALU.subtract), "T0", b)
                elif part[0] == "z" or part == "decay":
                    s = 1 if part == "decay" else int(part[1]) + 1
                    if s > 5:
                        return
                    if s <= 2:
                        gd.wait(pool, "qd1", b)
                    else:
                        gp.wait(pool, f"y{s - 2}", b)
                    gl.mark(pool.tensor_tensor(v8(gam[:, s % 2, :]), v8(Am[:, :]),
                                               mask_of(Lev[:, s * CHUNK:(s + 1) * CHUNK]), ALU.mult), f"X{s}", b)

            def scan_s(c):
                if c + 1 == SEQ // CHUNK:
                    return
                l0 = 32 * ((c + 1) % 2) + 4 * ((c + 1) // 2)
                sd_.wait(pool, "S", c)
                sl_.mark(pool.tensor_tensor(Sl[:, :].rearrange("p (h c) -> p h c", c=P),
                                            S[:, (c + 1) % 2, :].rearrange("p (h c) -> p h c", c=P),
                                            bc(lastb[:, l0:l0 + 4].unsqueeze(2), [P, 4, P]), ALU.mult), "Sl", c)

            gdn_order(prep, lambda c: None, scan_s, lambda part, e0, e1: None)
            tp.wait(pool, f"tr{TT - 1}")
            pool.memset(qO[0:SD, :, :], 0.0).then_inc(q_pad, 1)
            pool.wait_ge(q_odd, 1)
            pool.memset(qD[SD:P, :, :], 0.0).then_inc(q_pad, 1)
            for n in range(N_OUT + RING, N_FF):
                split_of(n)
            land0 = [have[i] for i in range(RING)]
            with pool.Fori(0, FFG) as g:
                for j in range(PER):
                    slot = (N_FF + j) % RING
                    if j == 0:
                        pool.wait_ge(down_out, g * 16 + 16 * (PAIRS_FF - 1))
                        free = (unit_done, g * 4 + UPS_FF)
                    elif j < RING:
                        free = (down_out, g * 16 + 16 * PAIRS_FF)
                    else:
                        free = (unit_done, g * 4 + (UPS_FF + j - RING + 1))
                    split(g * PER + (N_FF + j), slot, g * 32 + (have[slot] + 16 * (1 + j // RING)), free, 1024)

        def tap(u, k):
            return cols_t[:, k * 12 + u:k * 12 + u + 1]

        gO, gQ, gK, gXQ, gXK, gXKQ = (cols_t[:, c:c + 1] for c in (48, 53, 50, 54, 52, 55))

        def wcol(c0, n):
            return wba[:, :].rearrange("p (t c) -> p t c", c=24)[:, :, c0:c0 + n]

        def th(t, c0=0):
            return t[:, c0:c0 + 32].rearrange("p (t h) -> p t h", h=4)

        def rows_of(c):
            r0 = CHUNK * (c % 2)
            return c // 4, slice(r0, r0 + CHUNK), r0, 4 * ((c % 4) // 2)

        @block.tensor
        def _(pe):
            pe.wait_ge(consts, 1)
            for t in range(2):
                pe.wait_ge(nm_xn, t + 1)
                for j in range(2):
                    for k in range(4):
                        mm = pe.transpose(ps[:, 4 + 2 * t + j, k * P:(k + 1) * P],
                                          xn[:, t, (4 * j + k) * P:(4 * j + k + 1) * P], ident[:, :])
                    mm.then_inc(nm_tr, 1)
            for a in range(8):
                norm_pe_tile(pe, norm1, a)
                pe.wait_ge(nm_ev, 4)
                pe.wait_ge(kw_in[a % 2], 16 * (a // 2 + 1))
                if a >= 4:
                    pe.wait_ge(kv_ev, a - 3)
                for k in range(KT):
                    mm = pe.matmul(ps[:, 4 + a % 4, 0:N_MEM], KW[:, a % 2, k * P:(k + 1) * P], MT[:, k, :],
                                   start=(k == 0), stop=(k == KT - 1))
                mm.then_inc(kv_done, 1)
            pe.wait_ge(norm1.lo, 2 * TT)
            up_pe(pe, 0, HS, SEQ, N_SMALL)
            pe.wait_ge(kv_ev, 8)
            xka.wait(pe, "sq")
            for a in range(4):
                for mt in range(2):
                    mm = pe.matmul(ps[:, 6, 2 * a + mt:2 * a + mt + 1], sqk[:, a, mt * P:(mt + 1) * P],
                                   ones1[:, 0:1], start=True, stop=True)
            xkp.mark(mm, "stat")
            for mt in range(2):
                for a in range(4):
                    mm = pe.transpose(ps[:, 4 + mt, a * P:(a + 1) * P], vr[:, a, mt * P:(mt + 1) * P], ident[:, :])
                xkp.mark(mm, f"v{mt}")
            up_pe(pe, 1, HS, SEQ)
            xkd.wait(pe, "rs")
            for j in range(2):
                for q in range(4):
                    col = 4 * j + q
                    mm = pe.matmul(ps[:, 6 + j, q * P:(q + 1) * P], bc(rs[:, 64 + col:65 + col], [P, P]), ident[:, :],
                                   start=True, stop=True)
                xkp.mark(mm, f"bc{j}")
            xka.wait(pe, "v1")
            pe.wait_ge(small_ev, 2)
            for t in range(TT):
                mm = pe.transpose(ps[:, 4, t * 24:(t + 1) * 24], wT[0:24, t * P:(t + 1) * P], ident[0:24, 0:24])
            mm.then_inc(wba_tr, 1)
            pe.wait_ge(row_in, 16 * 10)
            pe.transpose(ps[:, 5, 0:53], stage[0:53, :], ident[0:53, 0:53]).then_inc(cols_ev, 1)
            up_pe(pe, 2, HS, SEQ)
            pe.wait_ge(wba_ev, 2)
            pe.wait_ge(cols_sb, 1)
            xkd.wait(pe, "n1")
            for a in range(8):
                pe.wait_ge(qi_lo, a + 1)

                def dots(i):
                    e = a * PER_A + i
                    _, j, t, c, w = entries[e]
                    if e >= 4:
                        pe.wait_ge(relu_out, e - 3)
                    for part in range(2):
                        mm = pe.matmul(ps[:, 4 + e % 4, 0:w], qI[:, a % 2, j, t * P:(t + 1) * P],
                                       kI[:, part, c:c + w], start=(part == 0), stop=(part == 1))
                    mm.then_inc(dots_out, 1)

                steps_k = HALVES * KT - 1

                def between(i):
                    for j in range(i * PER_A // steps_k, (i + 1) * PER_A // steps_k):
                        dots(j)
                up_pe(pe, a + 3, HS, SEQ, between=between)
            for u in range(2, 12):
                up_pe(pe, N_QKV + u, HS, SEQ)
                if u == 3:
                    pe.wait_ge(consts, 2)
                    g0d.wait(pe, "g")
                    for i, lhs in enumerate((Ublk[:, :], Mblk[:, :], half_ones[:, 0:P], half_ones[:, P:2 * P])):
                        mm = pe.matmul(ps[:, 5, 32 * i:32 * i + 32], lhs, gdec[:, :], start=True, stop=True)
                    g0p.mark(mm, "sums")
            for v in range(16):
                up_pe(pe, N_Z + v, HS, SEQ)
                if 3 <= v < 11:
                    u = v - 3
                    g0a.wait(pe, f"sq{u}")
                    for t in range(TT):
                        mm = pe.matmul(ps[:, 4, u * TT + t:u * TT + t + 1], sqg[:, t * P:(t + 1) * P],
                                       ones1[:, 0:1], start=True, stop=True)
                    g0p.mark(mm, f"st{u}")
                if v >= 12:
                    g0d.wait(pe, "rq")
                    g0a.wait(pe, "last")
                    for e in range(4 * (v - 12), 4 * (v - 12) + 4):
                        u, half = e // 2, e % 2
                        if e >= 4:
                            g0d.wait(pe, f"n{e - 4}")
                        for q in range(4):
                            col = u * TT + half * 4 + q
                            mm = pe.matmul(ps[:, 4 + e % 4, q * P:(q + 1) * P], bc(rs[:, col:col + 1], [P, P]),
                                           ident[:, :], start=True, stop=True)
                        g0p.mark(mm, f"bc{e}")
            meet(0, pe)

            def per_unit(b, fn):
                for ul in range(8):
                    for par in range(2):
                        r = slice(CHUNK * par, CHUNK * par + CHUNK)
                        mm = fn(ul, par, r)
                return mm

            def prep(b, part):
                B = b % 2
                if part == "in":
                    if b:
                        gd.wait(pe, "TT5", b - 1)
                        ga.wait(pe, "w1", b - 1)
                    for src, b0 in ((4, 0), (8, 2)):
                        for tl in range(2):
                            tok = slice((2 * b + tl) * P, (2 * b + tl + 1) * P)
                            for h in range(4):
                                mm = pe.transpose(ps[:, b0 + tl, h * P:(h + 1) * P], QKV[:, src + h, tok], ident[:, :])
                            gp.mark(mm, ("k" if src == 4 else "v") + str(tl), b)
                elif part == "gq":
                    gd.wait(pe, "kd1", b)

                    def gq(bank, src):
                        def fn(ul, par, r):
                            c0 = (2 * b + ul // 4) * P + par * CHUNK
                            c = slice(c0, c0 + CHUNK)
                            return pe.matmul(ps[r, bank, ul * CHUNK:(ul + 1) * CHUNK], QKV[:, 4 + ul % 4, c],
                                             QKV[:, src + ul % 4, c], start=True, stop=True)
                        return fn
                    per_unit(b, gq(0, 4))
                    gp.mark(per_unit(b, gq(1, 0)), "GQ", b)
                    gd.wait(pe, "vb1", b)
                    gl.wait(pe, "gU", b)
                    pe.matmul(ps[:, 2, :], Ublk[:, :], gMU[:, 0, :], start=True, stop=True)
                    gp.mark(pe.matmul(ps[:, 3, :], Mblk[:, :], gMU[:, 1, :], start=True, stop=True), "diff", b)
                elif part == "decay":
                    ga.wait(pe, "gQ", b)
                    for j in range(2):
                        for q in range(4):
                            col = 8 * b + 4 * j + q
                            mm = pe.matmul(ps[:, 2 + j, q * P:(q + 1) * P], bc(gdec[:, col:col + 1], [P, P]),
                                           Ublk[:, :], start=True, stop=True)
                        gp.mark(mm, f"db{j}", b)
                elif part == "x0":
                    gl.wait(pe, "X0", b)
                    gp.mark(per_unit(b, lambda ul, par, r: pe.matmul(
                        ps[r, 0, ul * CHUNK:(ul + 1) * CHUNK], Xm[r, ul * CHUNK:(ul + 1) * CHUNK], I64[r, :],
                        start=True, stop=True)), "x0", b)
                elif part[0] in "yz":
                    s = int(part[1])

                    def tri(bank, lhs, rhs):
                        return per_unit(b, lambda ul, par, r: pe.matmul(
                            ps[r, bank, ul * CHUNK:(ul + 1) * CHUNK], lhs[r, ul * CHUNK:(ul + 1) * CHUNK],
                            rhs[r, ul * CHUNK:(ul + 1) * CHUNK], start=True, stop=True))
                    if part[0] == "y":
                        gl.wait(pe, f"X{s}", b)
                        gd.wait(pe, f"TT{s - 1}", b)
                        gp.mark(tri(0, gam[:, s % 2, :], TTm[:, B, :]), f"y{s}", b)
                    else:
                        ga.wait(pe, f"y{s}", b)
                        if s > 1:
                            gd.wait(pe, f"T{s - 1}", b)
                        gp.mark(tri(1, Tm[:, :], Ym[:, :]), f"zt{s}", b)
                        if s < 5:
                            gp.mark(tri(2, Ym[:, :], Tm[:, :]), f"z{s}", b)
                elif part == "w":
                    gd.wait(pe, "TT5", b)
                    for ul in range(8):
                        for par in range(2):
                            r = slice(CHUNK * par, CHUNK * par + CHUNK)
                            c = slice(ul * CHUNK, (ul + 1) * CHUNK)
                            mm = pe.matmul(ps[:, 2 + par, c], nkbd[r, ul * P:(ul + 1) * P], TTm[r, B, c],
                                           start=True, stop=True)
                            if ul == 7:
                                gp.mark(mm, f"w{par}", b)

            def scan_v(c):
                b, r, r0, u0 = rows_of(c)
                B = b % 2
                if c % 4 == 0:
                    ga.wait(pe, "w1", b)
                    gd.wait(pe, "TT5", b)
                    gl.wait(pe, "X5", b)
                if c:
                    sa_.wait(pe, "vn", c - 1)
                for h in range(4):
                    mm = pe.matmul(ps[r, 4, h * P:(h + 1) * P], TTm[r, B, (u0 + h) * CHUNK:(u0 + h + 1) * CHUNK],
                                   vb[r, B, (u0 + h) * P:(u0 + h + 1) * P], start=(h == 0), stop=(c == 0 and h == 3),
                                   skip_group_check=True)
                if c:
                    sd_.wait(pe, "S", c - 1)
                    for h in range(4):
                        w0 = 8 * r0 + (u0 + h) * CHUNK
                        mm = pe.matmul(ps[r, 4, h * P:(h + 1) * P], wTt[:, B, w0:w0 + CHUNK],
                                       S[:, c % 2, h * P:(h + 1) * P], start=False, stop=(h == 3), skip_group_check=True)
                sp_.mark(mm, "v", c)
                if c:
                    sa_.wait(pe, "ot", c - 1)
                    for h in range(4):
                        w0 = (u0 + h) * P + r0
                        pe.matmul(ps[r, 5, h * P:(h + 1) * P], qdec[:, B, w0:w0 + CHUNK],
                                  S[:, c % 2, h * P:(h + 1) * P], start=(h == 0), stop=False, skip_group_check=True)

            def scan_s(c):
                b, r, r0, u0 = rows_of(c)
                B = b % 2
                sa_.wait(pe, "vn", c)
                for h in range(4):
                    mm = pe.matmul(ps[:, 6, h * P:(h + 1) * P], kdec[r, B, (u0 + h) * P:(u0 + h + 1) * P],
                                   vn[r, h * P:(h + 1) * P], start=True, stop=True)
                sp_.mark(mm, "s", c)
                for h in range(4):
                    mm = pe.matmul(ps[r, 5, h * P:(h + 1) * P], QKm[r, B, (u0 + h) * CHUNK:(u0 + h + 1) * CHUNK],
                                   vn[r, h * P:(h + 1) * P], start=(c == 0 and h == 0), stop=(h == 3),
                                   skip_group_check=True)
                sp_.mark(mm, "o", c)

            def dsa(part, e0, e1):
                for e in range(e0, e1):
                    u, src, half = half_unit(e)
                    if part == "sq":
                        d0a.wait(pe, f"sq{e}")
                        for q in range(4):
                            c = 2 * (u * TT + half * 4 + q)
                            mm = pe.matmul(ps[:, 7, c:c + 2], sqh[:, e % 2, q * P:(q + 1) * P], blk2[:, :],
                                           start=True, stop=True)
                        d0p.mark(mm, f"st{e}")
                    elif part == "bc":
                        d0d.wait(pe, "rs")
                        if e >= 4:
                            d0d.wait(pe, f"n{e - 4}")
                        for q in range(4):
                            c = 2 * (u * TT + half * 4 + q)
                            for j in range(2):
                                mm = pe.matmul(ps[SD * j:SD * (j + 1), e % 4, q * P:(q + 1) * P],
                                               bc(rs[:, c + j:c + j + 1], [P, SD]), ident[:, :], start=True, stop=True)
                        d0p.mark(mm, f"bc{e}")

            gdn_order(prep, scan_v, scan_s, dsa)
            meet(0, pe)
            pe.wait_ge(qk_in[2], 16)
            for t in range(TT):
                if t >= 2:
                    pe.wait_ge(v_ev, t - 1)
                for a in range(4):
                    mm = pe.transpose(ps[:, 6 + t % 2, a * P:(a + 1) * P], vraw[:, a, t * P:(t + 1) * P], ident[:, :])
                mm.then_inc(v_tr, 1)
            for t in range(TT):
                td.wait(pe, "on13")
                if t >= 4:
                    td.wait(pe, f"y{t - 4}")
                for h in range(4):
                    mm = pe.transpose(ps[:, t % 4, h * P:(h + 1) * P], QKV[:, h, t * P:(t + 1) * P], ident[:, :])
                tp.mark(mm, f"tr{t}")
            meet(0, pe)

            def logits(i):
                t, h = heads[i]
                if i >= 2:
                    pe.wait_ge(Lw, i - 1)
                for k, (c, w) in enumerate(chunks((t + 1) * P)):
                    mm = pe.matmul(ps[:, 2 * (i % 2) + k, 0:w], (qO if h % 2 else qD)[:, h // 2, t * P:(t + 1) * P],
                                   kD[:, h // 2, c:c + w], start=True, stop=True)
                mm.then_inc(lg, 1)

            def probs_tr(i):
                t, h = heads[i]
                pe.wait_ge(ex, i + 1)
                for k, (c, w) in enumerate(chunks((t + 1) * P)):
                    if ptc[i] + k >= 2:
                        pe.wait_ge(pte, ptc[i] + k - 1)
                    for q in range(w // P):
                        mm = pe.transpose(ps[:, 4 + (ptc[i] + k) % 2, q * P:(q + 1) * P],
                                          L[:, i % 3, c + q * P:c + (q + 1) * P], ident[:, :])
                    mm.then_inc(ptr, 1)

            def values(i):
                t, h = heads[i]
                pe.wait_ge(pte, ptc[i + 1])
                if h == 0 and t >= 2:
                    pe.wait_ge(dyb, t - 1)
                for s in range(t + 1):
                    mm = pe.matmul(ps[:, 6 + t % 2, h * SD:(h + 1) * SD], PT[:, i % 2, s * P:(s + 1) * P],
                                   vtok[:, s, h * SD:(h + 1) * SD], start=(s == 0), stop=(s == t))
                mm.then_inc(pvs, 1)

            def out_tr(t):
                pe.wait_ge(dnd, t + 1)
                for a in range(4):
                    mm = pe.transpose(ps[:, 6 + t % 2, a * P:(a + 1) * P], dtok[:, a * P:(a + 1) * P], ident[:, :])
                mm.then_inc(dtr, 1)

            N = len(heads)
            pe.wait_ge(q_pad, 2)
            logits(0)
            logits(1)
            for i in range(N):
                probs_tr(i)
                if i + 2 < N:
                    logits(i + 2)
                if i:
                    values(i - 1)
                if heads[i][1] == 4 and heads[i][0]:
                    out_tr(heads[i][0] - 1)
            values(N - 1)
            out_tr(TT - 1)
            meet(0, pe)

            def norm_beside(m):
                def after(r):
                    for t in ((), (0,), (1, 2), (3, 4))[r]:
                        norm_pe_tile(pe, m, t)
                return after

            def norm_after(m):
                for t in range(5, TT):
                    norm_pe_tile(pe, m, t)
                pe.wait_ge(m.lo, 2 * TT)

            for p in range(4):
                n = N_OUT + 2 * p
                down_pe(pe, [n % RING, (n + 1) % RING], n + 2, 16 * p if p else None,
                        lambda s, t: [HS[:, a, 2 * p + s, t * P:(t + 1) * P] for a in (0, 1)],
                        lambda s: pe.wait_ge(hs_lo, 2 * p + s + 1), norm_beside(norm2) if p == 3 else None)
            norm_after(norm2)
            def xq_sums(u):
                x0a.wait(pe, f"sq{u}")
                for t in range(TT):
                    mm = pe.matmul(ps[:, 4, u * TT + t:u * TT + t + 1], sqx[:, u, t * P:(t + 1) * P],
                                   ones1[:, 0:1], start=True, stop=True)
                x0p.mark(mm, f"st{u}")

            for u in range(4):
                up_pe(pe, N_KV + u, HS, SEQ)
                if u:
                    xq_sums(u - 1)
            pe.wait_ge(up_freed, ups[N_XO - 1] + 1)
            pe.wait_ge(kv_in, 16)

            def xlogits(t):
                if t >= 2:
                    pe.wait_ge(xex, 4 * (t - 1))
                for h in range(4):
                    b0 = 2 * (t % 2) + h // 2
                    mm = pe.matmul(ps[:, b0, (h % 2) * N_MEM:(h % 2 + 1) * N_MEM], qX[:, h, t * P:(t + 1) * P],
                                   kvX[:, 0, h * N_MEM:(h + 1) * N_MEM], start=True, stop=True)
                mm.then_inc(xlg, 1)

            xlogits(0)
            xq_sums(3)
            for t in range(TT):
                if t + 1 < TT:
                    xlogits(t + 1)
                if t == 0:
                    x0a.wait(pe, "sd")
                pe.wait_ge(xpn, t + 1)
                for j in range(2):
                    if t:
                        pe.wait_ge(xpte, 2 * (t - 1) + j + 1)
                    for q in range(4):
                        mm = pe.transpose(ps[:, 4 + j, q * P:(q + 1) * P],
                                          Pb[:, t % 2, (4 * j + q) * P:(4 * j + q + 1) * P], ident[:, :])
                    mm.then_inc(xptr, 1)
                if t % 4 == 3:
                    g = t // 4
                    pe.wait_ge(xpte, 2 * t + 2)
                    for h in range(4):
                        i = 4 * g + h
                        if i >= 2:
                            pe.wait_ge(xolo, i - 1)
                        for mt in range(2):
                            mm = pe.matmul(ps[:, 6 + i % 2, :], kvX[:, 1, mt * BANK + h * P:mt * BANK + (h + 1) * P], PTx[:, h, mt, :],
                                           start=(mt == 0), stop=(mt == 1))
                        mm.then_inc(xo_, 1)
            pe.wait_ge(xpte, 2 * TT)
            pe.wait_ge(xolo, 8)
            for p in range(2):
                n = N_XO + 2 * p
                down_pe(pe, [n % RING, (n + 1) % RING], n + 2, 16 * (4 + p),
                        lambda s, t: [HS[:, a, 2 * p + s, t * P:(t + 1) * P] for a in (0, 1)],
                        lambda s: None, norm_beside(norm3) if p else None)
            norm_after(norm3)
            with pe.Fori(0, FFG) as g:
                for j in range(4):
                    slot, b0 = (N_FF + j) % RING, 2 * (j % 2)
                    pe.wait_ge(w_split, g * PER + (N_FF + j + 1))
                    if j % 2 == 0:
                        pe.wait_ge(f_sil, g * 4 + (2 * (j // 2) + 1))
                    else:
                        pe.wait_ge(f_prod, g * 4 + (2 * (j // 2) + 1))
                    for half in range(HALVES):
                        c = slice(half * BANK, (half + 1) * BANK)
                        for k in range(KT):
                            hi, lo = (WS[:, slot, s, k * P:(k + 1) * P] for s in (0, 1))
                            pe.matmul(ps[:, b0 + half, :], lo, HS[:, 0, k, c], start=(k == 0), stop=False)
                            pe.matmul(ps[:, b0 + half, :], hi, HS[:, 1, k, c], start=False, stop=False)
                            mm = pe.matmul(ps[:, b0 + half, :], hi, HS[:, 0, k, c], start=False, stop=(k == KT - 1))
                    mm.then_inc(unit_done, 1)
                down_pe(pe, [(N_FF + 4) % RING, (N_FF + 5) % RING], g * PER + (N_FF + 6), g * 16 + 16 * PAIRS_FF,
                        lambda s, t: [AS[:, s, a, t * P:(t + 1) * P] for a in (0, 1)],
                        lambda s: pe.wait_ge(f_lo, g * 4 + (2 * s + 3)))

        @block.scalar
        def _(act):
            def clink(ins):
                link("a", act, a_chain, ins)

            act.wait_ge(consts, 1)
            act.wait_ge(m_in, 16)
            for t in range(2):
                act.activation(junk[:, t, :], M0[:, t, :], ACT.Square, accum_out=ss[:, 64 + t:65 + t]).then_inc(nm_ss, 1)
                act.wait_ge(nm_ss, t + 1)
                act.activation(sd[:, 64 + t:65 + t], ss[:, 64 + t:65 + t], ACT.Sqrt, bias=eps_t[:, 0:1],
                               scale=1.0 / D).then_inc(nm_sd, 1)

            def mem_act(t):
                if t == 0:
                    for i in range(4):
                        act.wait_ge(nm_tr, i + 1)
                        act.activation(MT[:, 4 * (i % 2):4 * (i % 2) + 4, (i // 2) * P:(i // 2 + 1) * P], blocks(4 + i),
                                       ACT.Copy).then_inc(nm_ev, 1)
                if t >= 2:
                    kv_act(t - 2)

            def kv_act(a):
                act.wait_ge(kv_done, a + 1)
                act.activation((kr if a < 4 else vr)[:, a % 4, :], ps[:, 4 + a % 4, 0:N_MEM], ACT.Copy).then_inc(kv_ev, 1)

            norm_act(act, norm1, mem_act)
            kv_act(6)
            kv_act(7)
            act.wait_ge(kv_ev, 4)
            act.wait_ge(nm_xn, 2)
            xka.mark(act.activation(sqk[:, :, :], kr[:, :, :], ACT.Square), "sq")
            act.wait_ge(unit_done, 1)
            for half in range(HALVES):
                c = slice(half * BANK, (half + 1) * BANK)
                act.activation(wT[0:24, c], ps[64:88, half, :], ACT.Copy)
                for r in (0, SD):
                    ins = act.activation(kI[r:r + SD, 0, c], ps[0:SD, half, :], ACT.Copy)
                ins.then_inc(small_ev, 1)
            xkp.wait(act, "stat")
            xka.mark(act.activation(sd[:, 64:72], ps[:, 6, 0:8], ACT.Sqrt, bias=eps_t[:, 0:1], scale=1.0 / GD), "sd")
            for mt in range(2):
                xkp.wait(act, f"v{mt}")
                xka.mark(act.activation(kv0[:, 1, mt * BANK:(mt + 1) * BANK], ps[:, 4 + mt, :], ACT.Copy), f"v{mt}")

            def queries(a):
                act.wait_ge(unit_done, a + 2)
                if a >= 2:
                    act.wait_ge(dots_out, (a - 1) * PER_A)
                for half in range(HALVES):
                    for j in range(2):
                        r = slice(SD * j, SD * j + SD)
                        ins = act.activation(qI[r, a % 2, j, half * BANK:(half + 1) * BANK],
                                             up_bank(a + 1, half)[r, :], ACT.Copy)
                    ins.then_inc(qi_hi, 1)

            queries(0)
            act.wait_ge(wba_tr, 1)
            w4 = ps[:, 4, 0:TT * 24].rearrange("p (t c) -> p t c", c=24)
            act.activation(wcol(0, IH), w4[:, :, 0:IH], ACT.Copy, scale=IH ** -0.5 * SD ** -0.5).then_inc(wba_ev, 1)
            act.activation(wcol(IH, 8), w4[:, :, IH:24], ACT.Copy).then_inc(wba_ev, 1)
            act.wait_ge(cols_ev, 1)
            act.activation(cols_t[:, 0:53], ps[:, 5, 0:53], ACT.Copy)
            act.activation(cols_t[:, 53:54], ps[:, 5, 49:50], ACT.Copy, scale=SD ** -0.5)
            act.activation(cols_t[:, 54:55], ps[:, 5, 51:52], ACT.Copy, scale=GD ** -0.5).then_inc(cols_sb, 1)
            for a in range(8):
                if a + 1 < 8:
                    queries(a + 1)
                for e in range(a * PER_A, (a + 1) * PER_A):
                    w = entries[e][4]
                    act.wait_ge(dots_out, e + 1)
                    if e >= 3:
                        act.wait_ge(acc_out, e - 2)
                    act.activation(relu[:, e % 3, 0:w], ps[:, 4 + e % 4, 0:w], ACT.Relu).then_inc(relu_out, 1)

            def silu_of(u):
                act.wait_ge(conv_ev, u + 1)
                act.activation(QKV[:, u, :], cacc[:, u % 2, :], ACT.Silu).then_inc(silu_ev, 1)

            act.wait_ge(acc_out, len(entries))
            act.wait_ge(kv_out, 16)
            for u in range(12):
                n = N_QKV + u
                act.wait_ge(unit_done, ups[n] + 1)
                if u >= 2:
                    act.wait_ge(conv_ev, u - 1)
                act.activation(raw[:, u % 2, 3:3 + BANK], up_bank(n, 0), ACT.Copy)
                act.activation(raw[:, u % 2, 3 + BANK:3 + SEQ], up_bank(n, 1), ACT.Copy).then_inc(up_freed, 1)
                if u == 1:
                    g0a.mark(act.activation(th(beta), wcol(16, 4), ACT.Sigmoid), "beta")
                    g0d.wait(act, "z")
                    g0a.mark(act.activation(gtmp[:, 32:64], gtmp[:, 0:32], ACT.Abs), "abs")
                    g0a.wait(act, "abs")
                    g0a.mark(act.activation(gtmp[:, 32:64], gtmp[:, 32:64], ACT.Exp, scale=-1.0), "exp")
                    g0a.wait(act, "exp")
                    g0a.mark(act.activation(gtmp[:, 32:64], gtmp[:, 32:64], ACT.Ln, bias=1.0), "ln")
                    g0a.mark(act.activation(alB[:, :], alB[:, :], ACT.Exp), "ea")
                if u:
                    silu_of(u - 1)
            silu_of(11)
            act.wait_ge(silu_ev, 12)
            for v in range(16):
                n = N_Z + v
                act.wait_ge(unit_done, ups[n] + 1)
                if v >= 2:
                    act.wait_ge(spilled[v % 2], 16 * (v // 2))
                for half in range(HALVES):
                    ins = act.activation(cacc[:, v % 2, half * BANK:(half + 1) * BANK], up_bank(n, half),
                                         ACT.Silu if v < 4 else ACT.Copy)
                ins.then_inc(up_freed, 1)
                act.wait_ge(up_freed, ups[n] + 1)
                act.dma_start(z_dram[v] if v < 4 else d_dram[v - 4], cacc[:, v % 2, :]).then_inc(spilled[v % 2], 16)
                if 2 <= v < 10:
                    if v > 2:
                        g0p.wait(act, f"st{v - 3}")
                    g0a.mark(act.activation(sqg[:, :], QKV[:, v - 2, :], ACT.Square), f"sq{v - 2}")
                if v == 10:
                    g0p.wait(act, "st7")
                    g0a.mark(act.activation(sd[:, 0:64], ps[:, 4, 0:64], ACT.Sqrt, bias=eps_t[:, 0:1]), "sd")
                    g0a.mark(act.activation(gtmp[:, 96:128], ps[:, 5, 0:32], ACT.Exp), "ed")
                    g0a.mark(act.activation(erem[:, :], ps[:, 5, 32:64], ACT.Exp), "erem")
                    g0a.mark(act.activation(lastb[:, :], ps[:, 5, 64:128], ACT.Exp), "last")
            for s in spilled:
                act.wait_ge(s, 16 * 8)
            meet(1, act)

            def prep(b, part):
                B = b % 2
                if part == "gq":
                    if b:
                        gp.wait(act, "w1", b - 1)
                    gp.wait(act, "diff", b)
                    ga.mark(act.activation(gam[:, 0, :], ps[:, 2, :], ACT.Exp), "gA", b)
                    ga.mark(act.activation(gam[:, 1, :], ps[:, 3, :], ACT.Exp), "gQ", b)
                elif part == "decay":
                    gd.wait(act, "Q1", b)
                    for j in range(2):
                        gp.wait(act, f"db{j}", b)
                        ga.mark(act.activation(gam[:, j, :], ps[:, 2 + j, :], ACT.Exp), f"e{j}", b)
                elif part[0] == "y":
                    gp.wait(act, part, b)
                    ga.mark(act.activation(Ym[:, :], ps[:, 0, :], ACT.Copy), part, b)
                elif part == "w":
                    if b >= 2:
                        sp_.wait(act, "o", 4 * (b - 1) - 1)
                    for j in range(2):
                        gp.wait(act, f"w{j}", b)
                        ga.mark(act.activation(wTt[:, B, j * BANK:(j + 1) * BANK], ps[:, 2 + j, :], ACT.Copy),
                                f"w{j}", b)

            def squares(t):
                sa_.wait(act, "ot", 2 * t + 1)
                if t:
                    ta.wait(act, f"q{t - 1}")
                for h in range(4):
                    ins = act.activation(gB[:, h * P:(h + 1) * P], QKV[:, h, t * P:(t + 1) * P], ACT.Square,
                                         accum_out=ss[:, 4 * t + h:4 * t + h + 1])
                ta.mark(ins, f"q{t}")

            def o_rms(i, t0, t1):
                ta.wait(act, f"q{t1 - 1}")
                ta.mark(act.activation(gtmp[:, 4 * t0:4 * t1], ss[:, 4 * t0:4 * t1], ACT.Sqrt, bias=eps_t[:, 0:1],
                                       scale=1.0 / GD), f"sd{i}")

            def dsa(part, e0, e1):
                if part == "on":
                    o_rms(0, 0, T_ON)
                elif part == "sq":
                    for e in range(e0, e1):
                        u, src, half = half_unit(e)
                        if e % 8 == 0:
                            act.wait_ge(qk_in[1 - e // 8], 16)
                        if e >= 2:
                            d0p.wait(act, f"st{e - 2}")
                        d0a.mark(act.activation(sqh[:, e % 2, :], src, ACT.Square), f"sq{e}")
                elif part == "sd":
                    d0p.wait(act, "st15")
                    d0a.mark(act.activation(sd[:, 0:128], ps[:, 7, 0:128], ACT.Sqrt, bias=eps_t[:, 0:1],
                                            scale=1.0 / SD), "sd")

            def scan_v(c):
                r = rows_of(c)[1]
                sp_.wait(act, "v", c)
                sa_.mark(act.activation(vn[r, :], ps[r, 4, :], ACT.Copy), "vn", c)
                if c and c % 2 == 0:
                    squares(c // 2 - 1)

            def scan_s(c):
                r, t = rows_of(c)[1], c // 2
                sp_.wait(act, "o", c)
                if c % 4 == 0:
                    gd.wait(act, "qd1", c // 4)
                sa_.mark(act.activation(QKV[r, 0:4, t * P:(t + 1) * P],
                                        ps[r, 5, :].rearrange("p (h c) -> p h c", c=P), ACT.Copy), "ot", c)

            gdn_order(prep, scan_v, scan_s, dsa)
            squares(TT - 1)
            o_rms(1, T_ON, TT)
            meet(1, act)
            for t in range(TT):
                act.wait_ge(v_tr, t + 1)
                act.activation(vtok[:, t, :], ps[:, 6 + t % 2, :], ACT.Copy).then_inc(v_ev, 1)
            tp.wait(act, f"tr{TT - 1}")
            act.activation(qO[SD:P, :, :], qD[SD:P, :, :], ACT.Copy).then_inc(q_odd, 1)
            meet(1, act)

            def exp_of(i):
                t, h = heads[i]
                n = (t + 1) * P
                act.wait_ge(mx, i + 1)
                if h == 0 and t >= 2:
                    act.wait_ge(drp, t - 1)
                act.activation(L[:, i % 3, 0:n], L[:, i % 3, 0:n], ACT.Exp, bias=sm8[:, i % 4:i % 4 + 1],
                               accum_out=sm8[:, 8 + 8 * (t % 2) + h:9 + 8 * (t % 2) + h]).then_inc(ex, 1)

            def pt_of(i):
                t, h = heads[i]
                if i >= 2:
                    act.wait_ge(pvs, i - 1)
                for k, (c, w) in enumerate(chunks((t + 1) * P)):
                    act.wait_ge(ptr, ptc[i] + k + 1)
                    act.activation(PT[:, i % 2, c:c + w], ps[:, 4 + (ptc[i] + k) % 2, 0:w], ACT.Copy).then_inc(pte, 1)

            N = len(heads)
            def y_tile(t):
                act.wait_ge(dtr, t + 1)
                act.activation(yB[:, :, t * P:(t + 1) * P], blocks(6 + t % 2), ACT.Copy).then_inc(dyb, 1)

            exp_of(0)
            for i in range(N):
                if i + 1 < N:
                    exp_of(i + 1)
                pt_of(i)
                if heads[i][1] == 5 and heads[i][0]:
                    y_tile(heads[i][0] - 1)
            y_tile(TT - 1)
            meet(1, act)

            for k in range(KT):
                src = yA[:, k, :] if k < 4 else yB[:, k - 4, :]
                act.activation(HS[:, 0, k, :], src, ACT.Copy).then_inc(hs_hi, 1)
            norm_act(act, norm2)
            for u in range(4):
                n = N_KV + u
                act.wait_ge(unit_done, ups[n] + 1)
                act.activation(qX[:, u, 0:BANK], up_bank(n, 0), ACT.Copy)
                act.activation(qX[:, u, BANK:SEQ], up_bank(n, 1), ACT.Copy).then_inc(up_freed, 1)
                act.wait_ge(up_freed, ups[n] + 1)
                x0a.mark(act.activation(sqx[:, u, :], qX[:, u, :], ACT.Square), f"sq{u}")
            x0p.wait(act, "st3")
            x0a.mark(act.activation(sd[:, 0:32], ps[:, 4, 0:32], ACT.Sqrt, bias=eps_t[:, 0:1], scale=1.0 / GD), "sd")

            def xprobs(t):
                act.wait_ge(xmx, t + 1)
                if t >= 2:
                    act.wait_ge(xptr, 2 * (t - 1))
                for h in range(4):
                    act.activation(Pb[:, t % 2, h * N_MEM:(h + 1) * N_MEM],
                                   ps[:, 2 * (t % 2) + h // 2, (h % 2) * N_MEM:(h % 2 + 1) * N_MEM], ACT.Exp,
                                   scale=rs[:, h * TT + t:h * TT + t + 1],
                                   bias=sm8[:, 4 * (t % 2) + h:4 * (t % 2) + h + 1],
                                   accum_out=sm8[:, 8 + 4 * (t % 2) + h:9 + 4 * (t % 2) + h]).then_inc(xex, 1)

            xprobs(0)
            for t in range(TT):
                if t + 1 < TT:
                    xprobs(t + 1)
                if t == 4:
                    act.wait_ge(xo_, 4)
                for j in range(2):
                    act.wait_ge(xptr, 2 * t + j + 1)
                    act.activation(PTx[:, 2 * j:2 * j + 2, :, (t % 4) * P:(t % 4 + 1) * P],
                                   ps[:, 4 + j, :].rearrange("p (h m c) -> p h m c", h=2, c=P), ACT.Copy).then_inc(xpte, 1)
                if t % 4 == 3:
                    for h in range(4):
                        i = t - 3 + h
                        act.wait_ge(xo_, i + 1)
                        act.activation(HS[:, 0, h, (t // 4) * BANK:(t // 4 + 1) * BANK], ps[:, 6 + i % 2, :],
                                       ACT.Copy).then_inc(xohi, 1)
            norm_act(act, norm3)
            for s in (f_sil, f_hi):
                act.sem_inc(s, 1)
            with act.Fori(0, FFG) as g:
                for f in range(2):
                    act.wait_ge(unit_done, g * 4 + (UPS_FF + 2 * f + 1))
                    act.wait_ge(f_prod, g * 4 + (2 * f + 1))
                    for half in range(HALVES):
                        c = slice(half * BANK, (half + 1) * BANK)
                        act.activation(sil[:, c], ps[:, half, :], ACT.Silu).then_inc(f_sil, 1)
                    act.wait_ge(down_out, g * 16 + 16 * PAIRS_FF)
                    for half in range(HALVES):
                        c = slice(half * BANK, (half + 1) * BANK)
                        act.wait_ge(f_prod, g * 4 + (2 * f + half + 2))
                        act.activation(AS[:, f, 0, c], prod[:, c], ACT.Copy).then_inc(f_hi, 1)

        @block.vector
        def _(dve):
            def clink(ins):
                link("d", dve, d_chain, ins)

            dve.wait_ge(gM_in, 16)
            for t in range(2):
                dve.wait_ge(nm_sd, t + 1)
                dve.reciprocal(rs[:, 64 + t:65 + t], sd[:, 64 + t:65 + t]).then_inc(nm_rs, 1)
                dve.wait_ge(nm_rs, t + 1)
                dve.scalar_tensor_tensor(xn[:, t, :], M0[:, t, :], rs[:, 64 + t:65 + t], gM[:, :],
                                         ALU.mult, ALU.mult).then_inc(nm_xn, 1)
            dve.wait_ge(nm_tr, 4)
            norm_dve(dve, norm1, 1)
            for half in range(HALVES):
                dve.wait_ge(small_ev, half + 1)
                c = slice(half * BANK, (half + 1) * BANK)
                for r in (0, SD):
                    ins = dve.tensor_tensor(kI[r:r + SD, 1, c], ps[0:SD, half, :], kI[0:SD, 0, c].bitcast(F32),
                                            ALU.subtract)
            ins.then_inc(up_freed, 1)

            def queries_lo(a):
                for half in range(HALVES):
                    c = slice(half * BANK, (half + 1) * BANK)
                    dve.wait_ge(qi_hi, 2 * a + half + 1)
                    for j in range(2):
                        r, o = slice(SD * j, SD * j + SD), slice(SD * (1 - j), SD * (2 - j))
                        ins = dve.tensor_tensor(qI[o, a % 2, j, c], up_bank(a + 1, half)[r, :],
                                                qI[r, a % 2, j, c].bitcast(F32), ALU.subtract)
                ins.then_inc(qi_lo, 1)
                dve.wait_ge(qi_lo, a + 1)
                dve.sem_inc(up_freed, 1)

            xka.wait(dve, "sd")
            xkd.mark(dve.reciprocal(rs[:, 64:72], sd[:, 64:72]), "rs")
            queries_lo(0)
            dve.wait_ge(wba_ev, 2)
            dve.wait_ge(cols_sb, 1)
            clink(dve.tensor_tensor(gXKQ, gXK, gXQ, ALU.mult))
            for j in range(2):
                xkp.wait(dve, f"bc{j}")
                xkd.mark(dve.scalar_tensor_tensor(kv0[:, 0, j * BANK:(j + 1) * BANK], kr[:, 2 * j:2 * j + 2, :].rearrange(
                    "p a c -> p (a c)"), gXKQ, ps[:, 6 + j, :], ALU.mult, ALU.mult), f"n{j}")
            for e, (a, j, t, c, w) in enumerate(entries):
                if e % PER_A == 0 and a + 1 < 8:
                    queries_lo(a + 1)
                acc = score[:, EOFF[t] + c:EOFF[t] + c + w]
                weight = wba[:, t * 24 + 2 * a + j:t * 24 + 2 * a + j + 1]
                dve.wait_ge(relu_out, e + 1)
                if e < PER_J:
                    dve.tensor_scalar(acc, relu[:, e % 3, 0:w], weight, None, ALU.mult).then_inc(acc_out, 1)
                else:
                    dve.wait_ge(acc_out, e + 1 - PER_J)
                    dve.scalar_tensor_tensor(acc, relu[:, e % 3, 0:w], weight, acc, ALU.mult,
                                             ALU.add).then_inc(acc_out, 1)
            dve.wait_ge(acc_out, len(entries))
            for t in range(TT):
                clink(dve.memset(score[0:CHUNK, EOFF[t + 1] - CHUNK:EOFF[t + 1]], TAKEN))
            clink(dve.memset(raw[:, 0, 0:3], 0.0))
            clink(dve.memset(raw[:, 1, 0:3], 0.0))

            taken = [0]

            def top_rounds(count):
                for i in range(taken[0], min(taken[0] + count, len(PAIRS) * ROUNDS)):
                    ts = PAIRS[i // ROUNDS]
                    for k, t in enumerate(ts):
                        if i:
                            dve.wait_ge(topk, 4 * i - 1 + k)
                        dve.max(top8[:, 8 * k:8 * k + 8], score[:, EOFF[t]:EOFF[t + 1]]).then_inc(topk, 1)
                    for k, t in enumerate(ts):
                        dve.wait_ge(topk, 4 * i + 1 + k)
                        s = score[:, EOFF[t]:EOFF[t + 1]]
                        dve.match_replace(s, top8[:, 8 * k:8 * k + 8], s, TAKEN).then_inc(topk, 1)
                    taken[0] = i + 1

            dve.wait_ge(cols_sb, 1)
            for u in range(12):
                dve.wait_ge(up_freed, ups[N_QKV + u] + 1)
                if u >= 2:
                    dve.wait_ge(silu_ev, u - 1)
                y, r = cacc[:, u % 2, :], raw[:, u % 2, :]
                clink(dve.tensor_scalar(y, r[:, 0:SEQ], tap(u, 0), None, ALU.mult))
                for k in range(1, 4):
                    ins = dve.scalar_tensor_tensor(y, r[:, k:k + SEQ], tap(u, k), y, ALU.mult, ALU.add)
                    if k < 3:
                        clink(ins)
                ins.then_inc(conv_ev, 1)
                if u == 0:
                    g0d.mark(dve.tensor_tensor(th(gtmp), wcol(20, 4), bc(dtB[:, :].unsqueeze(1), [P, TT, 4]), ALU.add), "z")
                    g0d.wait(dve, "z")
                    g0d.mark(dve.tensor_scalar(gtmp[:, 64:96], gtmp[:, 0:32], 0.0, None, ALU.max), "max")
                    g0d.wait(dve, "max")
                    g0a.wait(dve, "ln")
                    g0d.mark(dve.tensor_tensor(gtmp[:, 64:96], gtmp[:, 64:96], gtmp[:, 32:64], ALU.add), "sp")
                    g0d.wait(dve, "sp")
                    g0a.wait(dve, "ea")
                    g0d.mark(dve.scalar_tensor_tensor(th(gdec), th(gtmp, 64), -1.0, bc(alB[:, :].unsqueeze(1), [P, TT, 4]),
                                                      ALU.mult, ALU.mult), "g")
                top_rounds(2)
            def unit_norms(e0):
                for e in range(e0, e0 + 4):
                    u, c = e // 2, slice((e % 2) * BANK, (e % 2 + 1) * BANK)
                    g0p.wait(dve, f"bc{e}")
                    g0d.mark(dve.tensor_tensor(QKV[:, u, c], QKV[:, u, c], ps[:, 4 + e % 4, :], ALU.mult), f"n{e}")

            dve.wait_ge(consts, 2)
            clink(dve.scalar_tensor_tensor(negdist[:, :], negdist[:, :], -1.0, negdist[:, :], ALU.mult, ALU.min))
            clink(dve.memset(negdist[0:CHUNK, SEQ - CHUNK:SEQ], -BIG))
            for v in range(14):
                top_rounds(3)
                if v == 9:
                    g0a.wait(dve, "sd")
                    g0d.mark(dve.reciprocal(rs[:, 0:64], sd[:, 0:64]), "rs")
                    g0d.wait(dve, "rs")
                    g0d.mark(dve.tensor_scalar(rs[:, 0:32], rs[:, 0:32], GD ** -0.5, None, ALU.mult), "rq")
                    g0a.wait(dve, "ed")
                    g0d.mark(dve.scalar_tensor_tensor(nbed[:, :], gtmp[:, 96:128], -1.0, beta[:, :], ALU.mult,
                                                      ALU.mult), "nbed")
                if v >= 11:
                    unit_norms(4 * (v - 11))
            unit_norms(12)
            meet(2, dve)


            def v4(t, c0=0):
                return t[:, c0:c0 + 4 * P].rearrange("p (h c) -> p h c", c=P)

            def v8(ap):
                return ap.rearrange("p (u c) -> p u c", c=CHUNK)

            def prep(b, part):
                B = b % 2
                if part == "in":
                    if b >= 2:
                        sp_.wait(dve, "o", 4 * (b - 1) - 1)
                    if b:
                        gp.wait(dve, "w1", b - 1)
                    for tl in range(2):
                        sc = slice(8 * b + 4 * tl, 8 * b + 4 * tl + 4)
                        gp.wait(dve, f"k{tl}", b)
                        for dst, by, name in ((nkbd[:, tl * BANK:(tl + 1) * BANK], nbed, "nk"),
                                              (kdec[:, B, tl * BANK:(tl + 1) * BANK], erem, "kd")):
                            gd.mark(dve.tensor_tensor(v4(dst), v4(ps[:, tl, :]), bc(by[:, sc].unsqueeze(2), [P, 4, P]),
                                                      ALU.mult), f"{name}{tl}", b)
                    for tl in range(2):
                        sc = slice(8 * b + 4 * tl, 8 * b + 4 * tl + 4)
                        gp.wait(dve, f"v{tl}", b)
                        gd.mark(dve.tensor_tensor(v4(vb[:, B, tl * BANK:(tl + 1) * BANK]), v4(ps[:, 2 + tl, :]),
                                                  bc(beta[:, sc].unsqueeze(2), [P, 4, P]), ALU.mult), f"vb{tl}", b)
                elif part == "mask":
                    gp.wait(dve, "GQ", b)
                    ga.wait(dve, "gA", b)
                    gl.wait(dve, "bM", b)
                    gd.mark(dve.tensor_tensor(Am[:, :], ps[:, 0, :], gam[:, 0, :], ALU.mult), "A1", b)
                    ga.wait(dve, "gQ", b)
                    gd.mark(dve.tensor_tensor(QKm[:, B, :], ps[:, 1, :], gam[:, 1, :], ALU.mult), "Q1", b)
                elif part == "decay":
                    for j in range(2):
                        ga.wait(dve, f"e{j}", b)
                        tok = slice((2 * b + j) * P, (2 * b + j + 1) * P)
                        gd.mark(dve.tensor_tensor(v4(qdec[:, B, j * BANK:(j + 1) * BANK]), QKV[:, 0:4, tok],
                                                  v4(gam[:, j, :]), ALU.mult), f"qd{j}", b)
                    if b:
                        top_rounds(1)
                elif part == "x0":
                    gp.wait(dve, "x0", b)
                    gd.mark(dve.tensor_tensor(v8(TTm[:, B, :]), bc(I64[:, :].unsqueeze(1), [P, 8, CHUNK]),
                                              v8(ps[:, 0, :]), ALU.subtract), "TT0", b)
                    if b:
                        top_rounds(1)
                elif part[0] == "z":
                    s = int(part[1])
                    gp.wait(dve, f"zt{s}", b)
                    gd.wait(dve, f"TT{s - 1}", b)
                    gd.mark(dve.tensor_tensor(TTm[:, B, :], TTm[:, B, :], ps[:, 1, :], ALU.subtract), f"TT{s}", b)
                    if s < 5:
                        gp.wait(dve, f"z{s}", b)
                        gl.wait(dve, "T0", b)
                        if s > 1:
                            gd.wait(dve, f"T{s - 1}", b)
                        gd.mark(dve.tensor_tensor(Tm[:, :], Tm[:, :], ps[:, 2, :], ALU.subtract), f"T{s}", b)
                    top_rounds(1)

            def scan_v(c):
                pass

            def scan_s(c):
                sp_.wait(dve, "s", c)
                new = S[:, (c + 1) % 2, :]
                if c:
                    sl_.wait(dve, "Sl", c - 1)
                    sd_.mark(dve.tensor_tensor(new, Sl[:, :], ps[:, 6, :], ALU.add), "S", c)
                else:
                    sd_.mark(dve.tensor_copy(new, ps[:, 6, :]), "S", c)

            def scale_o(i, t0, t1):
                ta.wait(dve, f"sd{i}")
                td.mark(dve.reciprocal(gtmp[:, 32 + 4 * t0:32 + 4 * t1], gtmp[:, 4 * t0:4 * t1]), f"r{i}")
                td.wait(dve, f"r{i}")
                ro = gtmp[:, 32 + 4 * t0:32 + 4 * t1].rearrange("p (t h) -> p t h", h=4)
                for h in range(4):
                    o = QKV[:, h, t0 * P:t1 * P].rearrange("p (t c) -> p t c", c=P)
                    td.mark(dve.tensor_tensor(o, o, bc(ro[:, :, h:h + 1], [P, t1 - t0, P]), ALU.mult), f"on{i}{h}")

            def logit_bias(t):
                s = score[:, EOFF[t]:EOFF[t + 1]]
                nd = negdist[:, (TT - 1 - t) * P:SEQ]
                if (t + 1) * P <= TOPK:
                    clink(dve.tensor_copy(s, nd))
                else:
                    clink(dve.tensor_scalar(s, s, TAKEN, -BIG, ALU.is_gt, ALU.mult))
                    clink(dve.tensor_tensor(s, s, nd, ALU.add))

            def dsa(part, e0, e1):
                if part == "top":
                    top_rounds(2)
                elif part == "on":
                    top_rounds(len(PAIRS) * ROUNDS)
                    scale_o(0, 0, T_ON)
                elif part == "sq":
                    for t in range(e0 // 2, e1 // 2):
                        logit_bias(t)
                elif part == "sd":
                    d0a.wait(dve, "sd")
                    d0d.mark(dve.reciprocal(rs[:, :], sd[:, :]), "rs")
                elif part == "bc":
                    for e in range(e0, e1):
                        u, src, half = half_unit(e)
                        d0p.wait(dve, f"bc{e}")
                        d0d.mark(dve.scalar_tensor_tensor(src, src, gK if u < 4 else gQ, ps[:, e % 4, :],
                                                          ALU.mult, ALU.mult), f"n{e}")

            gdn_order(prep, scan_v, scan_s, dsa)
            meet(2, dve)
            scale_o(1, T_ON, TT)
            dve.wait_ge(z_in, 16)
            dve.wait_ge(v_tr, TT)
            for t in range(TT):
                tp.wait(dve, f"tr{t}")
                td.mark(dve.scalar_tensor_tensor(yA[:, :, t * P:(t + 1) * P], blocks(t % 4), gO,
                                                 zS[:, :, t * P:(t + 1) * P], ALU.mult, ALU.mult), f"y{t}")
            meet(2, dve)

            def out_tile(t):
                dve.wait_ge(pvs, SH * (t + 1))
                sums = sm8[:, 8 + 8 * (t % 2):16 + 8 * (t % 2)]
                dve.reciprocal(sm8[:, 24:32], sums).then_inc(drp, 1)
                dve.wait_ge(drp, t + 1)
                if t:
                    dve.wait_ge(dtr, t)
                dve.tensor_tensor(dtok[:, :].rearrange("p (h c) -> p h c", c=SD),
                                  ps[:, 6 + t % 2, :].rearrange("p (h c) -> p h c", c=SD),
                                  bc(sm8[:, 24:32].unsqueeze(2), [P, SH, SD]), ALU.mult).then_inc(dnd, 1)

            for i, (t, h) in enumerate(heads):
                n = (t + 1) * P
                dve.wait_ge(lg, i + 1)
                if i >= 3:
                    dve.wait_ge(ptr, ptc[i - 2])
                dve.scalar_tensor_tensor(L[:, i % 3, 0:n], score[:, EOFF[t]:EOFF[t + 1]], 2.0 ** -(h + 1),
                                         psf[:, 2 * (i % 2) * BANK:2 * (i % 2) * BANK + n], ALU.mult,
                                         ALU.add).then_inc(Lw, 1)
                dve.wait_ge(Lw, i + 1)
                if i >= 4:
                    dve.wait_ge(ex, i - 3)
                dve.tensor_reduce(sm8[:, i % 4:i % 4 + 1], L[:, i % 3, 0:n], AX, ALU.max, negate=True).then_inc(mx, 1)
                if h == 2 and t:
                    out_tile(t - 1)
            out_tile(TT - 1)
            meet(2, dve)

            def norm_beside(m, g_count):
                def after(t):
                    if t >= 2:
                        norm_dve_tile(dve, m, t - 2, g_count)
                return after

            def norm_after(m, g_count):
                for t in (TT - 2, TT - 1):
                    norm_dve_tile(dve, m, t, g_count)
                norm_dve_lo(dve, m, TT - 1)

            for k in range(KT):
                src = yA[:, k, :] if k < 4 else yB[:, k - 4, :]
                dve.wait_ge(hs_hi, k + 1)
                dve.tensor_tensor(HS[:, 1, k, :], src, HS[:, 0, k, :].bitcast(F32), ALU.subtract).then_inc(hs_lo, 1)
            dve.wait_ge(xr_in, 16)
            for p in range(4):
                down_dve(dve, 16 * p, first=(p == 0), after=norm_beside(norm2, 2) if p == 3 else None)
            norm_after(norm2, 2)
            x0a.wait(dve, "sd")
            x0d.mark(dve.reciprocal(rs[:, 0:32], sd[:, 0:32]), "rs")
            x0d.wait(dve, "rs")
            def xmax(t):
                dve.wait_ge(xlg, t + 1)
                if t >= 2:
                    dve.wait_ge(xex, 4 * (t - 1))
                raw_max = sm8[:, 32 + 4 * (t % 2):36 + 4 * (t % 2)]
                dve.tensor_reduce(raw_max, psf[:, 2 * (t % 2) * BANK:2 * (t % 2 + 1) * BANK].rearrange(
                    "p (h c) -> p h c", c=N_MEM), AX, ALU.max, negate=True).then_inc(x_max, 1)
                dve.wait_ge(x_max, t + 1)
                dve.tensor_tensor(sm8[:, 4 * (t % 2):4 * (t % 2) + 4], raw_max,
                                  rs[:, 0:32].rearrange("p (h t) -> p t h", t=TT)[:, t, :], ALU.mult).then_inc(xmx, 1)

            xmax(0)
            for t in range(TT):
                if t + 1 < TT:
                    xmax(t + 1)
                dve.wait_ge(xex, 4 * (t + 1))
                if t:
                    dve.wait_ge(xpn, t)
                dve.reciprocal(sm8[:, 24:28], sm8[:, 8 + 4 * (t % 2):12 + 4 * (t % 2)]).then_inc(xr, 1)
                dve.wait_ge(xr, t + 1)
                pv = Pb[:, t % 2, :].rearrange("p (h c) -> p h c", c=N_MEM)
                dve.tensor_tensor(pv, pv, bc(sm8[:, 24:28].unsqueeze(2), [P, 4, N_MEM]), ALU.mult).then_inc(xpn, 1)
                if t % 4 == 3:
                    for h in range(4):
                        i = t - 3 + h
                        c = slice((t // 4) * BANK, (t // 4 + 1) * BANK)
                        dve.wait_ge(xohi, i + 1)
                        dve.tensor_tensor(HS[:, 1, h, c], ps[:, 6 + i % 2, :], HS[:, 0, h, c].bitcast(F32),
                                          ALU.subtract).then_inc(xolo, 1)
            for p in range(2):
                down_dve(dve, 16 * (4 + p), after=norm_beside(norm3, 3) if p else None)
            norm_after(norm3, 3)
            for s in (f_prod, f_lo):
                dve.sem_inc(s, 1)
            with dve.Fori(0, FFG) as g:
                for f in range(2):
                    dve.wait_ge(unit_done, g * 4 + (UPS_FF + 2 * f + 2))
                    dve.wait_ge(f_hi, g * 4 + (2 * f + 1))
                    dve.wait_ge(f_lo, g * 4 + (2 * f + 1))
                    for half in range(HALVES):
                        c = slice(half * BANK, (half + 1) * BANK)
                        dve.wait_ge(f_sil, g * 4 + (2 * f + half + 2))
                        dve.tensor_tensor(prod[:, c], sil[:, c], ps[:, 2 + half, :], ALU.mult).then_inc(f_prod, 1)
                    for half in range(HALVES):
                        c = slice(half * BANK, (half + 1) * BANK)
                        dve.wait_ge(f_hi, g * 4 + (2 * f + half + 2))
                        dve.tensor_tensor(AS[:, f, 1, c], prod[:, c], AS[:, f, 0, c].bitcast(F32),
                                          ALU.subtract).then_inc(f_lo, 1)
                down_dve(dve, g * 16 + 16 * PAIRS_FF)


_INS = ["x", "mem", "g_mix", "w_in", "conv_w", "a_log", "dt_bias", "g_gdn_out", "g_q_dsa", "g_k_dsa", "w_out",
        "g_xattn", "g_mem", "w_xq", "w_xkv", "g_xq", "g_xk", "w_xo", "g_ffn", "w_gu", "w_down"]


def kernel(**inputs):
    import numpy as np
    import concourse.bacc as bacc
    from concourse.bass_utils import run_bass_kernel_spmd

    nc = bacc.Bacc("TRN2", target_bir_lowering=False, num_devices=1)
    arrays, args = {}, []
    for name in _INS:
        a = np.ascontiguousarray(inputs[name])
        arrays[f"in_{name}"] = a
        args.append(nc.dram_tensor(f"in_{name}", a.shape, mybir.dt.from_np(a.dtype), kind="ExternalInput").ap())
    out = nc.dram_tensor("out_0", (1, SEQ, D), F32, kind="ExternalOutput").ap()
    build_layer(nc, *args, out)
    r = run_bass_kernel_spmd(nc, [arrays], core_ids=[0])
    return r.results[0]["out_0"]
```
